# Optimizing a Trainium2 kernel written in Bass

```python
import jax, jax.numpy as jnp
from jax import lax
import numpy as np
import math

D_MODEL = 1024
BATCH = 1
SEQ = 1024
DEPTH = 2

GRID_W = 64
CTX_LEN = 256
EPS = 1e-6
ATTN_QBLOCK = 128
ROPE_BASE = 10000.0

MLA_HEADS = 8
MLA_Q_RANK = 384
MLA_KV_RANK = 256
MLA_NOPE = 64
MLA_ROPE = 32
MLA_V = 64
ROPE_PAIRS = MLA_ROPE // 4
MLSTM_HEADS = 4
MLSTM_DH = 128
MLSTM_CONV = 3
MLSTM_CHUNK = 64
GLA_HEADS = 4
GLA_DK = 64
GLA_DV = 128
GLA_GATE_RANK = 16
GLA_TAU = 16.0
GLA_CHUNK = 64
NA_HEADS = 8
NA_DH = 64
NA_KH = 8
NA_KW = 16

BRANCH_A = MLA_HEADS * MLA_V
BRANCH_B = MLSTM_HEADS * MLSTM_DH
BRANCH_C = GLA_HEADS * GLA_DV
BRANCH_D = NA_HEADS * NA_DH
EVEN_SPLITS = (MLA_Q_RANK, MLA_KV_RANK, MLA_ROPE, BRANCH_B, BRANCH_B, BRANCH_B, BRANCH_B, 4 * MLSTM_HEADS, BRANCH_A + BRANCH_B)
ODD_SPLITS = (GLA_HEADS * GLA_DK, GLA_HEADS * GLA_DK, BRANCH_C, 2 * GLA_GATE_RANK, BRANCH_D, BRANCH_D, BRANCH_D, BRANCH_C + BRANCH_D)
EVEN_IN = sum(EVEN_SPLITS)
ODD_IN = sum(ODD_SPLITS)


def split_cols(a, sizes):
    return jnp.split(a, np.cumsum(sizes)[:-1].tolist(), axis=-1)

def rmsnorm(x, g):
    xf = x.astype(jnp.float32)
    xf = xf * lax.rsqrt(jnp.mean(xf * xf, axis=-1, keepdims=True) + EPS)
    return xf.astype(x.dtype) * g

def head_rmsnorm(x, g, n_heads):
    B, T, W = x.shape
    return rmsnorm(x.reshape(B, T, n_heads, W // n_heads), g.reshape(n_heads, -1)).reshape(B, T, W)

def to_heads(a, n_heads):
    B, T, W = a.shape
    return a.reshape(B, T, n_heads, W // n_heads).transpose(0, 2, 1, 3)

def merge_heads(a):
    B, H, T, d = a.shape
    return a.transpose(0, 2, 1, 3).reshape(B, T, H * d)

def centred_dwconv(x, w, b):
    K = w.shape[0]
    T = x.shape[1]
    pad = K // 2
    xp = jnp.pad(x, ((0, 0), (pad, K - 1 - pad), (0, 0)))
    y = xp[:, 0:T] * w[0]
    for j in range(1, K):
        y = y + xp[:, j:j + T] * w[j]
    return y + b

def rope2d_tables(S):
    t = jnp.arange(S)
    inv = 1.0 / (ROPE_BASE ** (jnp.arange(ROPE_PAIRS, dtype=jnp.float32) / ROPE_PAIRS))
    ang = jnp.concatenate([(t // GRID_W)[:, None] * inv, (t % GRID_W)[:, None] * inv], axis=-1)
    return jnp.cos(ang), jnp.sin(ang)

def apply_rope2d(x, cos, sin):
    cos = cos.astype(x.dtype)
    sin = sin.astype(x.dtype)
    parts = []
    for a in range(2):
        y = x[..., a * 2 * ROPE_PAIRS:(a + 1) * 2 * ROPE_PAIRS]
        y1, y2 = y[..., :ROPE_PAIRS], y[..., ROPE_PAIRS:]
        ca = cos[:, a * ROPE_PAIRS:(a + 1) * ROPE_PAIRS]
        sa = sin[:, a * ROPE_PAIRS:(a + 1) * ROPE_PAIRS]
        parts += [y1 * ca - y2 * sa, y2 * ca + y1 * sa]
    return jnp.concatenate(parts, axis=-1)

def to_chunks(a, L):
    B, H, T = a.shape[:3]
    return jnp.moveaxis(a.reshape(B, H, T // L, L, *a.shape[3:]), 2, 0)

def from_chunks(a):
    nc, B, H, L = a.shape[:4]
    return jnp.moveaxis(a, 0, 2).reshape(B, H, nc * L, *a.shape[4:])

def block_attention(q, k, v, scale):
    B, H, S, dq = q.shape
    nb = S // ATTN_QBLOCK
    qb = jnp.moveaxis(q.reshape(B, H, nb, ATTN_QBLOCK, dq), 2, 0)

    def one_block(qi):
        s = jnp.einsum('bhqd,bhkd->bhqk', qi, k).astype(jnp.float32) * scale
        p = jax.nn.softmax(s, axis=-1).astype(v.dtype)
        return jnp.einsum('bhqk,bhkd->bhqd', p, v)

    o = lax.map(one_block, qb)
    return jnp.moveaxis(o, 0, 2).reshape(B, H, S, v.shape[-1])

def mlstm_chunked(q, k, v, ig, lf, state):
    L = MLSTM_CHUNK
    causal = jnp.tril(jnp.ones((L, L), dtype=bool))

    def step(carry, xs):
        C, n, m = carry
        qc, kc, vc, ic, fc = xs
        b = jnp.cumsum(fc, axis=-1)
        logw = jnp.where(causal, b[..., :, None] - b[..., None, :] + ic[..., None, :], -jnp.inf)
        inter = b + m[..., None]
        m_t = jnp.maximum(inter, jnp.max(logw, axis=-1))
        w_intra = jnp.exp(logw - m_t[..., None])
        w_inter = jnp.exp(inter - m_t)
        qk = jnp.einsum('bhtd,bhsd->bhts', qc, kc) * w_intra
        num = jnp.einsum('bhts,bhsv->bhtv', qk, vc) + w_inter[..., None] * jnp.einsum('bhtd,bhdv->bhtv', qc, C)
        den = jnp.sum(qk, axis=-1) + w_inter * jnp.einsum('bhtd,bhd->bht', qc, n)
        h = num / jnp.maximum(jnp.abs(den), jnp.exp(-m_t))[..., None]
        b_last = b[..., -1]
        logk = b_last[..., None] - b + ic
        m_new = jnp.maximum(b_last + m, jnp.max(logk, axis=-1))
        carry_decay = jnp.exp(b_last + m - m_new)
        kw = jnp.exp(logk - m_new[..., None])[..., None] * kc
        C = carry_decay[..., None, None] * C + jnp.einsum('bhsd,bhsv->bhdv', kw, vc)
        n = carry_decay[..., None] * n + jnp.sum(kw, axis=2)
        return (C, n, m_new), h

    xs = tuple(to_chunks(a.astype(jnp.float32), L) for a in (q, k, v, ig, lf))
    state, h = lax.scan(step, state, xs)
    return from_chunks(h), state

def gla_chunked(q, k, v, lg, S0):
    L = GLA_CHUNK
    causal = jnp.tril(jnp.ones((L, L), dtype=bool))

    def step(S, xs):
        qc, kc, vc, gc = xs
        bcum = jnp.cumsum(gc, axis=2)
        rel = bcum[:, :, :, None, :] - bcum[:, :, None, :, :]
        decay = jnp.exp(jnp.where(causal[:, :, None], rel, -jnp.inf))
        att = jnp.einsum('bhtd,bhsd,bhtsd->bhts', qc, kc, decay)
        o = jnp.einsum('bhts,bhsv->bhtv', att, vc) + jnp.einsum('bhtd,bhdv->bhtv', qc * jnp.exp(bcum), S)
        b_last = bcum[:, :, -1:]
        S_new = jnp.exp(b_last[:, :, 0])[..., None] * S + jnp.einsum('bhsd,bhsv->bhdv', kc * jnp.exp(b_last - bcum), vc)
        return S_new, o

    xs = tuple(to_chunks(a.astype(jnp.float32), L) for a in (q, k, v, lg))
    S, o = lax.scan(step, S0, xs)
    return from_chunks(o), S

def bidirectional_scan(chunk_fn, init_state, shared_c, gates_c, shared_l, gates_l):
    outs_c, outs_l = [], []
    for d in range(2):
        if d == 0:
            f = lambda a: a
        else:
            f = lambda a: jnp.flip(a, axis=2)
        hc, st = chunk_fn(*[f(a) for a in shared_c], *[f(g[d]) for g in gates_c], init_state)
        hl, _ = chunk_fn(*[f(a) for a in shared_l], *[f(g[d]) for g in gates_l], st)
        outs_c.append(f(hc))
        outs_l.append(f(hl))
    return outs_c[0] + outs_c[1], outs_l[0] + outs_l[1]

def neighbourhood_attention(q, k, v, k_ctx, v_ctx, rpb, rows):
    B, H, S, d = q.shape
    kh = min(NA_KH, rows)
    qg = q.reshape(B, H, rows, GRID_W, d)
    kg = k.reshape(B, H, rows, GRID_W, d)
    vg = v.reshape(B, H, rows, GRID_W, d)
    r_idx = jnp.arange(rows)
    c_idx = jnp.arange(GRID_W)
    win_rows = jnp.clip(r_idx - kh // 2, 0, rows - kh)[:, None] + jnp.arange(kh)
    win_cols = jnp.clip(c_idx - NA_KW // 2, 0, GRID_W - NA_KW)[:, None] + jnp.arange(NA_KW)
    dcol = win_cols - c_idx[:, None] + (NA_KW - 1)
    scale = d ** -0.5
    n_loc = kh * NA_KW

    def one_row(r):
        rws = win_rows[r]
        drow = rws - r + (NA_KH - 1)
        bias = rpb[:, drow[None, :, None], dcol[:, None, :]].astype(jnp.float32)
        qr = qg[:, :, r]
        kw = kg[:, :, rws][:, :, :, win_cols]
        vw = vg[:, :, rws][:, :, :, win_cols]
        s_loc = jnp.einsum('bhcd,bhicjd->bhcij', qr, kw).astype(jnp.float32) * scale + bias
        s_ctx = jnp.einsum('bhcd,bhnd->bhcn', qr, k_ctx).astype(jnp.float32) * scale
        logits = jnp.concatenate([s_loc.reshape(B, H, GRID_W, n_loc), s_ctx], axis=-1)
        p = jax.nn.softmax(logits, axis=-1).astype(v.dtype)
        p_loc = p[..., :n_loc].reshape(B, H, GRID_W, kh, NA_KW)
        return jnp.einsum('bhcij,bhicjd->bhcd', p_loc, vw) + jnp.einsum('bhcn,bhnd->bhcd', p[..., n_loc:], v_ctx)

    o = lax.map(one_row, r_idx)
    return jnp.moveaxis(o, 0, 2).reshape(B, H, S, d)

def mla_mlstm_mixer(u_lat, u_ctx, cos, sin, w_in, q_norm, w_uq, kv_norm, w_ukv, conv_w, conv_b, b_i, b_f, h_norm, w_out, need_ctx):
    def project(u, rotate):
        B, T, _ = u.shape
        cq, ckv, k_rope, mq, mk, mv, mo, gates, z = split_cols(u @ w_in, EVEN_SPLITS)
        q = to_heads(rmsnorm(cq, q_norm) @ w_uq, MLA_HEADS)
        kv = to_heads(rmsnorm(ckv, kv_norm) @ w_ukv, MLA_HEADS)
        q_nope, q_rope = q[..., :MLA_NOPE], q[..., MLA_NOPE:]
        k_nope, v = kv[..., :MLA_NOPE], kv[..., MLA_NOPE:]
        k_rope = k_rope[:, None]
        if rotate:
            q_rope = apply_rope2d(q_rope, cos, sin)
            k_rope = apply_rope2d(k_rope, cos, sin)
        q = jnp.concatenate([q_nope, q_rope], axis=-1)
        k = jnp.concatenate([k_nope, jnp.broadcast_to(k_rope, (B, MLA_HEADS, T, MLA_ROPE))], axis=-1)
        qk = jax.nn.silu(centred_dwconv(jnp.concatenate([mq, mk], axis=-1), conv_w, conv_b))
        mq = to_heads(qk[..., :BRANCH_B], MLSTM_HEADS) * MLSTM_DH ** -0.5
        mk = to_heads(qk[..., BRANCH_B:], MLSTM_HEADS)
        mv = to_heads(mv, MLSTM_HEADS)
        g = gates.reshape(B, T, 2, 2, MLSTM_HEADS).astype(jnp.float32)
        ig = (g[:, :, :, 0] + b_i).transpose(2, 0, 3, 1)
        lf = jax.nn.log_sigmoid(g[:, :, :, 1] + b_f).transpose(2, 0, 3, 1)
        return (q, k, v), (mq, mk, mv), (ig, lf), mo, z

    (qa_l, ka_l, va_l), seq_l, gates_l, mo_l, z_l = project(u_lat, True)
    (qa_c, ka_c, va_c), seq_c, gates_c, mo_c, z_c = project(u_ctx, False)
    scale = (MLA_NOPE + MLA_ROPE) ** -0.5
    a_lat = block_attention(qa_l, jnp.concatenate([ka_c, ka_l], axis=2), jnp.concatenate([va_c, va_l], axis=2), scale)
    B = u_lat.shape[0]
    init = (jnp.zeros((B, MLSTM_HEADS, MLSTM_DH, MLSTM_DH), jnp.float32),
            jnp.zeros((B, MLSTM_HEADS, MLSTM_DH), jnp.float32),
            jnp.zeros((B, MLSTM_HEADS), jnp.float32))
    h_c, h_l = bidirectional_scan(mlstm_chunked, init, seq_c, gates_c, seq_l, gates_l)

    def combine(a, h, mo, z, dtype):
        hm = head_rmsnorm(jax.nn.sigmoid(mo.astype(jnp.float32)) * merge_heads(h), h_norm, MLSTM_HEADS).astype(dtype)
        return (jnp.concatenate([merge_heads(a), hm], axis=-1) * jax.nn.silu(z)) @ w_out

    y_lat = combine(a_lat, h_l, mo_l, z_l, u_lat.dtype)
    y_ctx = None
    if need_ctx:
        y_ctx = combine(block_attention(qa_c, ka_c, va_c, scale), h_c, mo_c, z_c, u_ctx.dtype)
    return y_lat, y_ctx

def gla_na_mixer(u_lat, u_ctx, rows, w_in, w_gate, b_gate, gla_norm, rpb, w_out, need_ctx):
    def project(u):
        B, T, _ = u.shape
        gq, gk, gv, ga, nq, nk, nv, z = split_cols(u @ w_in, ODD_SPLITS)
        ga = ga.reshape(B, T, 2, GLA_GATE_RANK)
        lg = jax.nn.log_sigmoid(jnp.einsum('btdr,drk->dbtk', ga, w_gate).astype(jnp.float32) + b_gate[:, None, None]) / GLA_TAU
        lg = lg.reshape(2, B, T, GLA_HEADS, GLA_DK).transpose(0, 1, 3, 2, 4)
        seq = (to_heads(gq, GLA_HEADS) * GLA_DK ** -0.5, to_heads(gk, GLA_HEADS), to_heads(gv, GLA_HEADS))
        na = (to_heads(nq, NA_HEADS), to_heads(nk, NA_HEADS), to_heads(nv, NA_HEADS))
        return seq, (lg,), na, z

    seq_l, gates_l, (nq_l, nk_l, nv_l), z_l = project(u_lat)
    seq_c, gates_c, (nq_c, nk_c, nv_c), z_c = project(u_ctx)
    B = u_lat.shape[0]
    init = jnp.zeros((B, GLA_HEADS, GLA_DK, GLA_DV), jnp.float32)
    o_c, o_l = bidirectional_scan(gla_chunked, init, seq_c, gates_c, seq_l, gates_l)
    na_l = neighbourhood_attention(nq_l, nk_l, nv_l, nk_c, nv_c, rpb, rows)

    def combine(o, na, z, dtype):
        g = head_rmsnorm(merge_heads(o), gla_norm, GLA_HEADS).astype(dtype)
        return (jnp.concatenate([g, merge_heads(na)], axis=-1) * jax.nn.silu(z)) @ w_out

    y_lat = combine(o_l, na_l, z_l, u_lat.dtype)
    y_ctx = None
    if need_ctx:
        y_ctx = combine(o_c, block_attention(nq_c, nk_c, nv_c, NA_DH ** -0.5), z_c, u_ctx.dtype)
    return y_lat, y_ctx

def first_inputs(seed: int = 0) -> dict:
    key = jax.random.key(seed)
    keys = iter(jax.random.split(key, 32))

    def rnd(shape, s):
        return jax.random.normal(next(keys), shape, jnp.float32) * s

    def gain(n):
        return 1.0 + rnd((n,), 0.05)

    D = D_MODEL
    return {
        'x': rnd((BATCH, SEQ, D), 1.0),
        'c': rnd((BATCH, D), 1.0),
        'ctx': rnd((BATCH, CTX_LEN, D), 1.0),
        'c_ctx': rnd((D,), 1.0),
        'l0_norm': gain(D),
        'l0_w_mod': rnd((D, 3 * D), 0.5 * D ** -0.5),
        'l0_b_mod': rnd((3 * D,), 0.02),
        'l0_w_in': rnd((D, EVEN_IN), D ** -0.5),
        'l0_mla_q_norm': gain(MLA_Q_RANK),
        'l0_mla_w_uq': rnd((MLA_Q_RANK, MLA_HEADS * (MLA_NOPE + MLA_ROPE)), MLA_Q_RANK ** -0.5),
        'l0_mla_kv_norm': gain(MLA_KV_RANK),
        'l0_mla_w_ukv': rnd((MLA_KV_RANK, MLA_HEADS * (MLA_NOPE + MLA_V)), MLA_KV_RANK ** -0.5),
        'l0_mlstm_conv_w': rnd((MLSTM_CONV, 2 * BRANCH_B), MLSTM_CONV ** -0.5),
        'l0_mlstm_conv_b': rnd((2 * BRANCH_B,), 0.02),
        'l0_mlstm_b_i': rnd((2, MLSTM_HEADS), 0.1),
        'l0_mlstm_b_f': jnp.linspace(3.0, 6.0, MLSTM_HEADS)[None] + rnd((2, MLSTM_HEADS), 0.1),
        'l0_mlstm_norm': gain(BRANCH_B),
        'l0_w_out': rnd((BRANCH_A + BRANCH_B, D), (BRANCH_A + BRANCH_B) ** -0.5),
        'l1_norm': gain(D),
        'l1_w_mod': rnd((D, 3 * D), 0.5 * D ** -0.5),
        'l1_b_mod': rnd((3 * D,), 0.02),
        'l1_w_in': rnd((D, ODD_IN), D ** -0.5),
        'l1_gla_w_gate': rnd((2, GLA_GATE_RANK, GLA_HEADS * GLA_DK), GLA_GATE_RANK ** -0.5),
        'l1_gla_b_gate': rnd((2, GLA_HEADS * GLA_DK), 0.5),
        'l1_gla_norm': gain(BRANCH_C),
        'l1_na_rpb': rnd((NA_HEADS, 2 * NA_KH - 1, 2 * NA_KW - 1), 0.1),
        'l1_w_out': rnd((BRANCH_C + BRANCH_D, D), (BRANCH_C + BRANCH_D) ** -0.5),
        'final_norm': gain(D),
    }

def first_block(x, c, ctx, c_ctx,
              l0_norm, l0_w_mod, l0_b_mod, l0_w_in, l0_mla_q_norm, l0_mla_w_uq, l0_mla_kv_norm, l0_mla_w_ukv,
              l0_mlstm_conv_w, l0_mlstm_conv_b, l0_mlstm_b_i, l0_mlstm_b_f, l0_mlstm_norm, l0_w_out,
              l1_norm, l1_w_mod, l1_b_mod, l1_w_in, l1_gla_w_gate, l1_gla_b_gate, l1_gla_norm, l1_na_rpb, l1_w_out,
              final_norm):
    S = x.shape[1]
    rows = S // GRID_W
    cos, sin = rope2d_tables(S)
    norms = (l0_norm, l1_norm)
    mods = ((l0_w_mod, l0_b_mod), (l1_w_mod, l1_b_mod))
    mixer_params = (
        (l0_w_in, l0_mla_q_norm, l0_mla_w_uq, l0_mla_kv_norm, l0_mla_w_ukv, l0_mlstm_conv_w, l0_mlstm_conv_b,
         l0_mlstm_b_i, l0_mlstm_b_f, l0_mlstm_norm, l0_w_out),
        (l1_w_in, l1_gla_w_gate, l1_gla_b_gate, l1_gla_norm, l1_na_rpb, l1_w_out),
    )
    h_lat, h_ctx = x, ctx
    for layer in range(DEPTH):
        need_ctx = layer < DEPTH - 1
        w_mod, b_mod = mods[layer]
        shift_l, scale_l, gate_l = jnp.split(jax.nn.silu(c) @ w_mod + b_mod, 3, axis=-1)
        shift_c, scale_c, gate_c = jnp.split(jax.nn.silu(c_ctx) @ w_mod + b_mod, 3, axis=-1)
        u_lat = rmsnorm(h_lat, norms[layer]) * (1 + scale_l[:, None]) + shift_l[:, None]
        u_ctx = rmsnorm(h_ctx, norms[layer]) * (1 + scale_c) + shift_c
        if layer % 2 == 0:
            y_lat, y_ctx = mla_mlstm_mixer(u_lat, u_ctx, cos, sin, *mixer_params[layer], need_ctx=need_ctx)
        else:
            y_lat, y_ctx = gla_na_mixer(u_lat, u_ctx, rows, *mixer_params[layer], need_ctx=need_ctx)
        h_lat = h_lat + gate_l[:, None] * y_lat
        if need_ctx:
            h_ctx = h_ctx + gate_c * y_ctx
    return rmsnorm(h_lat, final_norm)


DEPTH_2 = 1

N_MEM = 256
MEM_HEADS = 4
MEM_HEAD_DIM = 128
MEM_WIDTH = MEM_HEADS * MEM_HEAD_DIM
D_RNN = 3 * D_MODEL // 4
LRU_BLOCK = 64
N_LRU_BLOCKS = D_RNN // LRU_BLOCK
CONV_WIDTH = 4
LRU_C = 8.0
DIL_GROUPS = ((128, 1), (512, 4), (2048, 16))
N_DIL_GROUPS = len(DIL_GROUPS)
HEADS_PER_GROUP = 4
DIL_HEAD_DIM = 64
N_DIL_HEADS = N_DIL_GROUPS * HEADS_PER_GROUP
DIL_QKV_WIDTH = 3 * N_DIL_HEADS * DIL_HEAD_DIM
DIL_OUT_WIDTH = HEADS_PER_GROUP * DIL_HEAD_DIM
NUM_BUCKETS = 32
MAX_DISTANCE = 2048
N_BRANCHES = 3
D_FF = 4 * D_MODEL
NEG = -1e30

SPLITS = (D_RNN, 2 * D_RNN, 2 * D_RNN + DIL_QKV_WIDTH, 2 * D_RNN + DIL_QKV_WIDTH + MEM_WIDTH)
D_IN = 2 * D_RNN + DIL_QKV_WIDTH + MEM_WIDTH + N_BRANCHES * D_MODEL


def _rmsnorm(x, g):
    x32 = x.astype(jnp.float32)
    y = x32 * lax.rsqrt(jnp.mean(x32 * x32, axis=-1, keepdims=True) + EPS)
    return (y * g.astype(jnp.float32)).astype(x.dtype)

def _t5_bucket(dist):
    max_exact = NUM_BUCKETS // 2
    df = jnp.maximum(dist, 1).astype(jnp.float32)
    large = max_exact + (jnp.log(df / max_exact) / math.log(MAX_DISTANCE / max_exact)
                         * (NUM_BUCKETS - max_exact)).astype(jnp.int32)
    large = jnp.minimum(large, NUM_BUCKETS - 1)
    return jnp.where(dist < max_exact, dist, large)

def _rg_lru(xc, w_a, b_a, w_x, b_x, lam):
    B, S, C = xc.shape
    xb = xc.reshape(B, S, N_LRU_BLOCKS, LRU_BLOCK)
    r = jax.nn.sigmoid((jnp.einsum('bshi,hij->bshj', xb, w_a).reshape(B, S, C) + b_a).astype(jnp.float32))
    i = jax.nn.sigmoid((jnp.einsum('bshi,hij->bshj', xb, w_x).reshape(B, S, C) + b_x).astype(jnp.float32))
    log_a = -LRU_C * r * jax.nn.softplus(-lam.astype(jnp.float32))
    a = jnp.exp(log_a)
    mult = jnp.sqrt(-jnp.expm1(2.0 * log_a))
    b = mult * (i * xc.astype(jnp.float32))

    def combine(left, right):
        a1, b1 = left
        a2, b2 = right
        return a1 * a2, a2 * b1 + b2

    _, h = lax.associative_scan(combine, (a, b), axis=1)
    return h

def _dilated_group(q, k, v, table_g, dilation, span):
    B, S, H, Dh = q.shape
    L = S // dilation
    nb = -(-L // span)
    Lp = nb * span

    def to_blocks(t):
        t = t.reshape(B, L, dilation, H, Dh).transpose(0, 2, 3, 1, 4)
        t = jnp.pad(t, ((0, 0), (0, 0), (0, 0), (0, Lp - L), (0, 0)))
        return t.reshape(B, dilation, H, nb, span, Dh)

    def with_prev(t):
        prev = jnp.pad(t, ((0, 0), (0, 0), (0, 0), (1, 0), (0, 0), (0, 0)))[:, :, :, :-1]
        return jnp.concatenate([prev, t], axis=-2)

    qb = to_blocks(q)
    kk = with_prev(to_blocks(k))
    vv = with_prev(to_blocks(v))

    qi = jnp.arange(span)[:, None]
    kj = jnp.arange(2 * span)[None, :]
    off = qi + span - kj
    valid = (off >= 0) & (off <= span)
    mask = valid[None] & ((jnp.arange(nb)[:, None, None] > 0) | (kj >= span)[None])
    bucket = _t5_bucket(jnp.maximum(off, 0) * dilation)
    bias = jnp.transpose(table_g.astype(jnp.float32)[bucket], (2, 0, 1))

    s = jnp.einsum('brhnqc,brhnkc->brhnqk', qb, kk) * (DIL_HEAD_DIM ** -0.5) + bias[None, None, :, None]
    s = jnp.where(mask[None, None, None], s, NEG)
    m = jnp.max(s, axis=-1, keepdims=True)
    p = jnp.exp(s - m)
    den = jnp.sum(p, axis=-1)
    o = jnp.einsum('brhnqk,brhnkc->brhnqc', p, vv) / den[..., None]
    lse = m[..., 0] + jnp.log(den)

    o = o.reshape(B, dilation, H, Lp, Dh)[:, :, :, :L].transpose(0, 3, 1, 2, 4).reshape(B, S, H, Dh)
    lse = lse.reshape(B, dilation, H, Lp)[:, :, :, :L].transpose(0, 3, 1, 2).reshape(B, S, H)
    return o, lse

def second_inputs(seed: int = 0) -> dict:
    key = jax.random.key(seed)
    ks = jax.random.split(key, 24)
    f32 = jnp.float32

    def nrm(k, shape, fan_in):
        return jax.random.normal(k, shape, f32) * (fan_in ** -0.5)

    def gain(k, n):
        return 1.0 + 0.05 * jax.random.normal(k, (n,), f32)

    u = jax.random.uniform(ks[11], (D_RNN,), f32, 0.9, 0.999)
    sig = u ** (1.0 / LRU_C)
    lam = jnp.log(sig) - jnp.log1p(-sig)
    return {
        "x": jax.random.normal(ks[0], (BATCH, SEQ, D_MODEL), f32),
        "mem": jax.random.normal(ks[1], (BATCH, N_MEM, D_MODEL), f32),
        "g_mix": gain(ks[2], D_MODEL),
        "w_in": nrm(ks[3], (D_MODEL, D_IN), D_MODEL),
        "b_gate": 0.01 * jax.random.normal(ks[4], (N_BRANCHES * D_MODEL,), f32),
        "conv_w": nrm(ks[5], (CONV_WIDTH, D_RNN), CONV_WIDTH),
        "conv_b": 0.01 * jax.random.normal(ks[6], (D_RNN,), f32),
        "w_rg_a": nrm(ks[7], (N_LRU_BLOCKS, LRU_BLOCK, LRU_BLOCK), LRU_BLOCK),
        "b_rg_a": 0.01 * jax.random.normal(ks[8], (D_RNN,), f32),
        "w_rg_x": nrm(ks[9], (N_LRU_BLOCKS, LRU_BLOCK, LRU_BLOCK), LRU_BLOCK),
        "b_rg_x": 0.01 * jax.random.normal(ks[10], (D_RNN,), f32),
        "lru_lambda": lam,
        "w_lru_out": nrm(ks[12], (D_RNN, D_MODEL), D_RNN),
        "rel_bias": 0.1 * jax.random.normal(ks[13], (NUM_BUCKETS, N_DIL_HEADS), f32),
        "w_dil_out": nrm(ks[14], (DIL_OUT_WIDTH, D_MODEL), DIL_OUT_WIDTH),
        "g_mem": gain(ks[15], D_MODEL),
        "w_mem_kv": nrm(ks[16], (D_MODEL, 2 * MEM_WIDTH), D_MODEL),
        "w_mem_out": nrm(ks[17], (MEM_WIDTH, D_MODEL), MEM_WIDTH),
        "w_out": nrm(ks[18], (D_MODEL, D_MODEL), D_MODEL),
        "g_mlp": gain(ks[19], D_MODEL),
        "w_mlp_in": nrm(ks[20], (D_MODEL, D_FF), D_MODEL),
        "w_mlp_out": nrm(ks[21], (D_FF, D_MODEL), D_FF),
        "g_final": gain(ks[22], D_MODEL),
    }

def second_block(x, mem, g_mix, w_in, b_gate, conv_w, conv_b, w_rg_a, b_rg_a, w_rg_x, b_rg_x,
              lru_lambda, w_lru_out, rel_bias, w_dil_out, g_mem, w_mem_kv, w_mem_out, w_out,
              g_mlp, w_mlp_in, w_mlp_out, g_final):
    B, S, D = x.shape
    dt = x.dtype
    f32 = jnp.float32
    mem_n = _rmsnorm(mem, g_mem)

    for _ in range(DEPTH_2):
        h = _rmsnorm(x, g_mix)
        proj = h @ w_in
        x_lru, gate_lru, qkv, q_mem, gates = jnp.split(proj, SPLITS, axis=-1)

        xc = lax.conv_general_dilated(x_lru, conv_w[:, None, :].astype(x_lru.dtype), window_strides=(1,),
                                      padding=[(CONV_WIDTH - 1, 0)], dimension_numbers=('NWC', 'WIO', 'NWC'),
                                      feature_group_count=D_RNN) + conv_b
        hl = _rg_lru(xc, w_rg_a, b_rg_a, w_rg_x, b_rg_x, lru_lambda)
        y_lru = (jax.nn.gelu(gate_lru.astype(f32)) * hl).astype(dt) @ w_lru_out

        qkv = qkv.astype(f32).reshape(B, S, 3, N_DIL_GROUPS, HEADS_PER_GROUP, DIL_HEAD_DIM)
        outs, lses = [], []
        for g, (window, dil) in enumerate(DIL_GROUPS):
            o_g, lse_g = _dilated_group(qkv[:, :, 0, g], qkv[:, :, 1, g], qkv[:, :, 2, g],
                                        rel_bias[:, g * HEADS_PER_GROUP:(g + 1) * HEADS_PER_GROUP],
                                        dil, window // dil)
            outs.append(o_g)
            lses.append(lse_g)
        alpha = jax.nn.softmax(jnp.stack(lses, axis=0), axis=0)
        o_dil = jnp.sum(alpha[..., None] * jnp.stack(outs, axis=0), axis=0)
        y_dil = o_dil.reshape(B, S, DIL_OUT_WIDTH).astype(dt) @ w_dil_out

        kv = (mem_n @ w_mem_kv).astype(f32).reshape(B, N_MEM, 2, MEM_HEADS, MEM_HEAD_DIM)
        qm = q_mem.astype(f32).reshape(B, S, MEM_HEADS, MEM_HEAD_DIM)
        sm = jnp.einsum('bqhc,bkhc->bhqk', qm, kv[:, :, 0]) * (MEM_HEAD_DIM ** -0.5)
        pm = jax.nn.softmax(sm, axis=-1)
        om = jnp.einsum('bhqk,bkhc->bqhc', pm, kv[:, :, 1]).reshape(B, S, MEM_WIDTH)
        y_mem = om.astype(dt) @ w_mem_out

        gt = jax.nn.sigmoid((gates + b_gate).astype(f32)).reshape(B, S, N_BRANCHES, D)
        merged = (gt[:, :, 0] * y_lru.astype(f32) + gt[:, :, 1] * y_dil.astype(f32)
                  + gt[:, :, 2] * y_mem.astype(f32)).astype(dt)
        x = x + merged @ w_out

        hm = _rmsnorm(x, g_mlp)
        x = x + jnp.square(jax.nn.relu(hm @ w_mlp_in)) @ w_mlp_out

    return _rmsnorm(x, g_final)


def setup_inputs(seed=0):
    out = dict(first_inputs(seed))
    for name, value in second_inputs(seed + 1).items():
        if name != "x":
            out[name + "_2"] = value
    return out


def reference(
    x, c, ctx, c_ctx, l0_norm, l0_w_mod, l0_b_mod, l0_w_in, l0_mla_q_norm, l0_mla_w_uq,
    l0_mla_kv_norm, l0_mla_w_ukv, l0_mlstm_conv_w, l0_mlstm_conv_b, l0_mlstm_b_i, l0_mlstm_b_f,
    l0_mlstm_norm, l0_w_out, l1_norm, l1_w_mod, l1_b_mod, l1_w_in, l1_gla_w_gate, l1_gla_b_gate,
    l1_gla_norm, l1_na_rpb, l1_w_out, final_norm, mem_2, g_mix_2, w_in_2, b_gate_2, conv_w_2,
    conv_b_2, w_rg_a_2, b_rg_a_2, w_rg_x_2, b_rg_x_2, lru_lambda_2, w_lru_out_2, rel_bias_2,
    w_dil_out_2, g_mem_2, w_mem_kv_2, w_mem_out_2, w_out_2, g_mlp_2, w_mlp_in_2, w_mlp_out_2,
    g_final_2,
):
    x = first_block(
        x, c, ctx, c_ctx, l0_norm, l0_w_mod, l0_b_mod, l0_w_in, l0_mla_q_norm, l0_mla_w_uq,
        l0_mla_kv_norm, l0_mla_w_ukv, l0_mlstm_conv_w, l0_mlstm_conv_b, l0_mlstm_b_i,
        l0_mlstm_b_f, l0_mlstm_norm, l0_w_out, l1_norm, l1_w_mod, l1_b_mod, l1_w_in,
        l1_gla_w_gate, l1_gla_b_gate, l1_gla_norm, l1_na_rpb, l1_w_out, final_norm,
    )
    return second_block(
        x, mem_2, g_mix_2, w_in_2, b_gate_2, conv_w_2, conv_b_2, w_rg_a_2, b_rg_a_2, w_rg_x_2,
        b_rg_x_2, lru_lambda_2, w_lru_out_2, rel_bias_2, w_dil_out_2, g_mem_2, w_mem_kv_2,
        w_mem_out_2, w_out_2, g_mlp_2, w_mlp_in_2, w_mlp_out_2, g_final_2,
    )


_drawn_inputs = setup_inputs


def setup_inputs(seed=0):
    import zlib

    import numpy as np

    out = dict(_drawn_inputs(seed))
    spreads = {}
    factors = {'l0_norm': 5.104,
     'l0_b_mod': 2.871,
     'l0_mla_q_norm': 8.0,
     'l0_mla_w_uq': 4.925,
     'l0_mla_kv_norm': 8.0,
     'l0_mlstm_conv_b': 8.0,
     'l0_mlstm_b_i': 8.0,
     'l0_mlstm_norm': 6.343,
     'l1_norm': 3.585,
     'l1_b_mod': 3.457,
     'l1_gla_norm': 7.071,
     'l1_na_rpb': 8.0,
     'g_mix_2': 2.896,
     'b_gate_2': 23.756,
     'conv_b_2': 2.951,
     'b_rg_a_2': 57.2,
     'b_rg_x_2': 54.913,
     'rel_bias_2': 8.0,
     'g_mem_2': 8.0,
     'g_mlp_2': 4.398}
    for name, (base, spread) in spreads.items():
        noise = np.random.default_rng([zlib.crc32(name.encode()), seed]).standard_normal(out[name].shape)
        drawn = base * np.exp(spread * noise) if base else spread * noise
        out[name] = __import__('jax').numpy.asarray(drawn.astype(out[name].dtype))
    for name, factor in factors.items():
        out[name] = (out[name] * factor).astype(out[name].dtype)
    return out
```

```python
import math
from contextlib import ExitStack

import numpy as np

import concourse.bass as bass
from concourse import mybir

F32 = mybir.dt.float32
ALU = mybir.AluOpType
ACT = mybir.ActivationFunctionType
AX = mybir.AxisListType.X

P = 128
D = 1024
KD = D // P
NCTX, NLAT = 256, 1024
T = NCTX + NLAT
TT = T // P
EPS = 1e-6
NEG = -1e30
WORDS = 51200



class Memory:
    whole, top = None, 0
    held, sems = None, []
    stored, stored_before = None, 0


def clear_semaphores(nc, sems):
    with nc.Block() as block:
        @block.sync
        def _(sp):
            for x in sems:
                sp.sem_clear(x)


def give_back_semaphores(nc):
    clear_semaphores(nc, Memory.sems)
    Memory.held.close()
    Memory.sems = []


class Stage:

    def __init__(self, nc, name, turn=False):
        if not turn and len(Memory.sems) > 90:
            give_back_semaphores(nc)
        self.nc, self.name, self.stack, self.sems = nc, name, ExitStack(), []

    def __enter__(self):
        self.stack.__enter__()
        self.bottom = Memory.top
        return self

    def __exit__(self, *e):
        Memory.top = self.bottom
        return self.stack.__exit__(*e)

    def sb(self, name, shape, dt=F32):
        words = 1
        for n in shape[1:]:
            words *= n
        a = Memory.whole[0:shape[0], Memory.top:Memory.top + words]
        Memory.top += -(-words // 8) * 8
        assert Memory.top <= WORDS, (self.name, name, Memory.top)
        dims = " ".join(f"d{n}" for n in range(len(shape) - 1))
        return a.rearrange(f"p ({dims}) -> p {dims}", **{f"d{n}": w for n, w in enumerate(shape[1:])})

    def ps(self, name, shape, dt=F32):
        return self.stack.enter_context(self.nc.psum_tensor(f"{self.name}_{name}", shape, dt))

    def sem(self, name):
        self.sems.append(Memory.held.enter_context(self.nc.semaphore(f"{self.name}_{name}")))
        Memory.sems.append(self.sems[-1])
        return self.sems[-1]

    def reset(self):
        clear_semaphores(self.nc, self.sems)

    def block(self):
        return self.stack.enter_context(self.nc.Block())


def chunks(t0, tn, w=512):
    return [(t0 + o, min(w, tn - o)) for o in range(0, tn, w)]


def modulation(nc, name, cc_dram, w_dram, b_dram, mod):
    MT = 3 * D // P
    with Stage(nc, name) as s:
        cc = s.sb("cc", [P, KD * 2])
        sc = s.sb("silu", [P, KD, 2])
        b = s.sb("b", [P, MT])
        NB = 6
        w = s.sb("w", [P, NB, KD * P])
        acc = s.ps("acc", [P, MT, 2])
        in_sem, silu_sem = s.sem("in"), s.sem("silued")
        w_ready, w_free = [s.sem(f"w_ready{b}") for b in range(NB)], s.sem("w_free")
        block = s.block()

        @block.sync
        def _(sp):
            sp.dma_start(cc[:], cc_dram).then_inc(in_sem, 16)
            sp.dma_start(b[:], b_dram).then_inc(in_sem, 16)
            for j in range(MT):
                if j >= NB:
                    sp.wait_ge(w_free, j - NB + 1)
                sp.dma_start(w[:, j % NB, :], w_dram[j * P:(j + 1) * P, :]).then_inc(w_ready[j % NB], 16)

        @block.scalar
        def _(act):
            act.wait_ge(in_sem, 32)
            nc.scalar.activation(sc[:].rearrange("p a b -> p (a b)"), cc[:], ACT.Silu).then_inc(silu_sem, 1)

        @block.tensor
        def _(pe):
            pe.wait_ge(silu_sem, 1)
            for j in range(MT):
                pe.wait_ge(w_ready[j % NB], 16 * (j // NB + 1))
                for k in range(KD):
                    last = nc.tensor.matmul(acc[:, j, :], w[:, j % NB, k * P:(k + 1) * P], sc[:, k, :],
                                            start=k == 0, stop=k == KD - 1)
                last.then_inc(w_free, 1)

        @block.vector
        def _(dve):
            dve.wait_ge(in_sem, 32)
            dve.wait_ge(w_free, MT)
            for v in range(2):
                nc.vector.tensor_tensor(mod[:, :, v], acc[:, :, v], b[:], ALU.add)


def norm_scales(nc, name, g_dram, mod, gain):
    with Stage(nc, name) as s:
        g = s.sb("g", [P, KD])
        g_sem = s.sem("g")
        block = s.block()

        @block.sync
        def _(sp):
            sp.dma_start(g[:], g_dram).then_inc(g_sem, 16)

        @block.vector
        def _(dve):
            dve.wait_ge(g_sem, 16)
            for v in range(2):
                nc.vector.tensor_scalar(gain[:, :, v], mod[:, KD:2 * KD, v], 1.0, None, ALU.add)
                dve.drain()
                nc.vector.tensor_tensor(gain[:, :, v], gain[:, :, v], g[:], ALU.mult)


def rmsnorm(nc, name, x, kt, width, parts, out, ones, g_dram=None, eps_col=None):
    t_lo = min(p[0] for p in parts)
    t_n = sum(p[1] for p in parts)
    with Stage(nc, name) as s:
        sq = s.sb("sq", [P, 2, T])
        rinv = s.sb("rinv", [P, T])
        g = s.sb("g", [P, kt])
        ssum = s.ps("ssum", [P, 3 * 512])
        g_sem, sq_sem, mm_sem, root_sem = s.sem("g_in"), s.sem("squared"), s.sem("summed"), s.sem("root")
        r_sem, u_sem = s.sem("rinv_ready"), s.sem("scaled")
        block = s.block()
        sl = slice(t_lo, t_lo + t_n)

        @block.sync
        def _(sp):
            if g_dram is not None:
                sp.dma_start(g[:], g_dram).then_inc(g_sem, 16)

        @block.scalar
        def _(act):
            for k in range(kt):
                if k >= 2:
                    act.wait_ge(mm_sem, k - 1)
                nc.scalar.activation(sq[:, k % 2, 0:t_n], x[:, k, sl], ACT.Square).then_inc(sq_sem, 1)
            act.wait_ge(mm_sem, kt)
            nc.scalar.activation(rinv[:, 0:t_n], ssum[:, 0:t_n], ACT.Sqrt, bias=eps_col,
                                 scale=1.0 / width).then_inc(root_sem, 1)
            for k in range(kt):
                for t0, tn, gain, shift in parts:
                    if shift is not None:
                        act.wait_ge(u_sem, k + 1)
                        nc.scalar.activation(out[:, k, t0:t0 + tn], out[:, k, t0:t0 + tn], ACT.Identity,
                                             bias=shift[:, k:k + 1])

        @block.tensor
        def _(pe):
            for k in range(kt):
                pe.wait_ge(sq_sem, k + 1)
                for o, n in chunks(0, t_n):
                    last = nc.tensor.matmul(ssum[:, o:o + n], ones[:], sq[:, k % 2, o:o + n],
                                            start=k == 0, stop=k == kt - 1)
                last.then_inc(mm_sem, 1)

        @block.vector
        def _(dve):
            dve.wait_ge(root_sem, 1)
            if g_dram is not None:
                dve.wait_ge(g_sem, 16)
            nc.vector.reciprocal(rinv[:, 0:t_n], rinv[:, 0:t_n])
            dve.drain()
            for k in range(kt):
                for t0, tn, gain, shift in parts:
                    gn = g if gain is None else gain
                    last = nc.vector.scalar_tensor_tensor(
                        out=out[:, k, t0:t0 + tn], in0=x[:, k, t0:t0 + tn], scalar=gn[:, k:k + 1],
                        in1=rinv[:, t0 - t_lo:t0 - t_lo + tn], op0=ALU.mult, op1=ALU.mult)
                last.then_inc(u_sem, 1)


def gemm_fm(nc, name, x, kt, t0, tn, w_dram, mt, out_dram=None, out_sb=None, relu2=False, acc=None, gate=None):
    assert mt % 2 == 0
    nb = len(chunks(0, tn))
    with Stage(nc, name) as s:
        w = s.sb("w", [P, 2, kt * P])
        ev = s.sb("ev", [P, 2, tn]) if out_dram is not None or relu2 else None
        prod = s.ps("prod", [P, 2, nb * 512])
        w_ready, w_free = [s.sem(f"w_ready{b}") for b in range(2)], s.sem("w_free")
        mm_done, ps_free = s.sem("mm_done"), s.sem("ps_free")
        stored = [s.sem(f"stored{b}") for b in range(2)]
        block = s.block()

        def products(pe, b):
            for o, n in chunks(0, tn):
                for k in range(kt):
                    last = nc.tensor.matmul(prod[:, b, o:o + n], w[:, b, k * P:(k + 1) * P],
                                            x[:, k, t0 + o:t0 + o + n], start=k == 0, stop=k == kt - 1)
            last.then_inc(w_free, 1)
            return last

        if out_dram is not None:
            @block.sync
            def _(sp):
                with sp.Fori(0, mt // 2) as i:
                    for b in range(2):
                        sp.wait_ge(w_free, 2 * i + b + 1)
                        sp.wait_ge(w_free, 1)
                        sp.dma_start(w[:, b, :], w_dram[bass.ds(i * 2 * P + b * P, P), :]).then_inc(w_ready[b], 16)

            @block.tensor
            def _(pe):
                pe.sem_inc(w_free, 2)
                with pe.Fori(0, mt // 2) as i:
                    for b in range(2):
                        pe.wait_ge(w_ready[b], 16 * i + 16)
                        pe.wait_ge(ps_free, 2 * i + b + 1)
                        products(pe, b)

            @block.scalar
            def _(act):
                act.sem_inc(ps_free, 2)
                for b in range(2):
                    act.sem_inc(stored[b], 16)
                with act.Fori(0, mt // 2) as i:
                    for b in range(2):
                        act.wait_ge(w_free, 2 * i + b + 3)
                        act.wait_ge(stored[b], 16 * i + 16)
                        nc.scalar.activation(ev[:, b, :], prod[:, b, 0:tn], ACT.Copy).then_inc(ps_free, 1)
                        act.drain()
                        act.dma_start(out_dram[bass.ds(i * 2 * P + b * P, P), :], ev[:, b, :]).then_inc(stored[b], 16)
                for b in range(2):
                    act.wait_ge(stored[b], 8 * mt + 16)
        else:
            @block.sync
            def _(sp):
                for j in range(mt):
                    if j >= 2:
                        sp.wait_ge(w_free, j - 1)
                    sp.dma_start(w[:, j % 2, :], w_dram[j * P:(j + 1) * P, :]).then_inc(w_ready[j % 2], 16)

            @block.tensor
            def _(pe):
                for j in range(mt):
                    pe.wait_ge(w_ready[j % 2], 16 * (j // 2 + 1))
                    if j >= 2:
                        pe.wait_ge(ps_free, j - 1)
                    products(pe, j % 2)

            @block.scalar
            def _(act):
                if relu2:
                    for j in range(mt):
                        act.wait_ge(w_free, j + 1)
                        if j >= 2:
                            act.wait_ge(mm_done, j - 1)
                        nc.scalar.activation(ev[:, j % 2, :], prod[:, j % 2, 0:tn], ACT.Relu).then_inc(ps_free, 1)

            @block.vector
            def _(dve):
                for j in range(mt):
                    if relu2:
                        dve.wait_ge(ps_free, j + 1)
                        nc.vector.tensor_tensor(out_sb[:, j, 0:tn], ev[:, j % 2, :], ev[:, j % 2, :],
                                                ALU.mult).then_inc(mm_done, 1)
                        continue
                    dve.wait_ge(w_free, j + 1)
                    if acc is None:
                        nc.vector.tensor_copy(out_sb[:, j, 0:tn], prod[:, j % 2, 0:tn]).then_inc(ps_free, 1)
                        continue
                    for c0, cn, g in gate:
                        last = nc.vector.scalar_tensor_tensor(
                            out=acc[:, j, c0:c0 + cn], in0=prod[:, j % 2, c0 - t0:c0 - t0 + cn],
                            scalar=1.0 if g is None else g[:, j:j + 1], in1=acc[:, j, c0:c0 + cn],
                            op0=ALU.mult, op1=ALU.add)
                    last.then_inc(ps_free, 1)


def gemm_tm(nc, name, x, kt, t0, tn, w_dram, n, out_dram):
    with Stage(nc, name) as s:
        w = s.sb("w", [P, kt, n])
        ev = s.sb("ev", [P, 2, n])
        cols = chunks(0, n)
        prod = s.ps("prod", [P, 2, len(cols) * 512])
        w_sem, mm, free = s.sem("w_in"), s.sem("mm"), s.sem("copied")
        stored = [s.sem(f"stored{b}") for b in range(2)]
        block = s.block()

        @block.sync
        def _(sp):
            sp.dma_start(w[:].rearrange("p k n -> p (k n)"), w_dram).then_inc(w_sem, 16)

        @block.tensor
        def _(pe):
            pe.wait_ge(w_sem, 16)
            for j in range(tn // P):
                if j >= 2:
                    pe.wait_ge(free, j - 1)
                for o, m in cols:
                    for k in range(kt):
                        last = nc.tensor.matmul(prod[:, j % 2, o:o + m], x[:, k, t0 + j * P:t0 + (j + 1) * P],
                                                w[:, k, o:o + m], start=k == 0, stop=k == kt - 1)
                last.then_inc(mm, 1)

        @block.scalar
        def _(act):
            for j in range(tn // P):
                act.wait_ge(mm, j + 1)
                if j >= 2:
                    act.wait_ge(stored[j % 2], 16 * (j // 2))
                nc.scalar.activation(ev[:, j % 2, :], prod[:, j % 2, 0:n], ACT.Copy).then_inc(free, 1)
                act.drain()
                act.dma_start(out_dram[j * P:(j + 1) * P, :], ev[:, j % 2, :]).then_inc(stored[j % 2], 16)
            for b in range(2):
                act.wait_ge(stored[b], 8 * (tn // P))


class Unit:

    def __init__(self, q, keys, vt, out, bias=None):
        self.q, self.keys, self.vt, self.out, self.bias = q, keys, vt, out, bias
        self.nk = sum(n for _, n in keys)
        assert self.nk == P * len(vt)


def attention(nc, name, heads, dk, dv, scale, units, q_dram, k_dram, v_load, v_loads, nvt, out_dram, out_w, ident,
              tq, tk, stats=False, bias_shape=None, bias_load=None, bias_loads=0, bias_fill=(), rope=None):
    nu = len(units)
    U = 2 * nu
    groups = [(b, u, g) for b in range(2) for u in range(nu) for g in range((len(units[u].vt) + 3) // 4)]
    NG = len(groups)
    gpos = {bug: n for n, bug in enumerate(groups)}
    ev_n = [sum(1 for n in range(NG) if n % 2 == p) for p in range(2)]

    def evs(n):
        return n // 2

    assert NG % 2 == 0
    krows = dk if rope is None else dk - 32
    biased = bias_shape is not None
    with Stage(nc, name) as s:
        q = s.sb("q", [P, 2, tq])
        k = s.sb("k", [P, 2, tk])
        v = s.sb("v", [P, 2, nvt, dv])
        nkmax = max(u.nk for u in units)
        pr = s.sb("probs", [P, 2, nkmax])
        prT = s.sb("probsT", [P, 2, nkmax])
        sco = s.sb("scores", [P, 2, nkmax]) if biased else None
        bias = s.sb("bias", [P, 2] + list(bias_shape)) if biased else None
        negm = s.sb("negm", [P, 5])
        sums = s.sb("sums", [P, 4])
        rinv = s.sb("rinv", [P, 4])
        osb = s.sb("osb", [P, 4, out_w])
        packed = nkmax > 2 * 512
        S = s.ps("S", [P, 2, (3 if packed else 2) * 512])
        TR = s.ps("TR", [P, 2, 4, P])
        O = S[:, :, 1280:1280 + dv] if packed else s.ps("O", [P, 2, 512])[:, :, 0:dv]
        assert not packed or nkmax + dv <= 3 * 512
        loaded = [s.sem(f"loaded{b}") for b in range(2)]
        prepared, scored, maxed, exped, trans = (s.sem(x) for x in ("prepared", "scored", "maxed", "exped", "trans"))
        copied = [s.sem(f"copied{p}") for p in range(2)]
        pv, oready = s.sem("pv_done"), s.sem("out_ready")
        out_free = s.sem("out_free")
        stored, before = Memory.stored, Memory.stored_before
        Memory.stored_before += heads // 2 * nu * 16 * len(out_dram(0, 0))
        const_in = s.sem("const_in")
        if rope is not None:
            qsw = s.sb("qsw", [P, 2, tq])
            tab = s.sb("tab", [P, 2, tk])
            ksw = s.sb("ksw", [P, tk])
            assert dk == 96
        nload = 2 + v_loads + bias_loads + (4 if rope is not None else 0)
        if rope is not None:
            nload = 2 + v_loads + 4
        block = s.block()
        R = slice(64, 96)

        @block.sync
        def _(sp):
            if rope is not None:
                kr, cs = rope
                for a in range(2):
                    sp.dma_start(tab[R, a, :], cs[a * 32:(a + 1) * 32, :]).then_inc(const_in, 16)
                for b in range(2):
                    sp.dma_start(k[R, b, :], kr).then_inc(const_in, 16)
                for g in range(4):
                    o = (g ^ 1) * 8
                    sp.dma_start(ksw[64 + 8 * g:72 + 8 * g, :], kr[o:o + 8, :]).then_inc(const_in, 16)
            with sp.Fori(0, heads // 2) as i:
                for b in range(2):
                    h = 2 * i + b
                    sp.wait_ge(pv, i * U + (b + 1) * nu)
                    sp.wait_ge(prepared, 1)
                    sp.dma_start(q[0:dk, b, :], q_dram[bass.ds(i * (2 * dk) + b * dk, dk), :]).then_inc(loaded[b], 16)
                    sp.dma_start(k[0:krows, b, :], k_dram[bass.ds(i * (2 * krows) + b * krows, krows), :]).then_inc(loaded[b], 16)
                    v_load(sp, h, v[:, b], loaded[b])
                    if biased:
                        bias_load(sp, h, bias[:, b], loaded[b])
                    if rope is not None:
                        for g in range(4):
                            sp.dma_start(qsw[64 + 8 * g:72 + 8 * g, b, :],
                                         q_dram[bass.ds(i * (2 * dk) + b * dk + 64 + (g ^ 1) * 8, 8), :]).then_inc(loaded[b], 16)

        @block.tensor
        def _(pe):
            pe.sem_inc(pv, U)

            def scores(i, b, u):
                n = b * nu + u
                if u == 0:
                    if rope is not None:
                        pe.wait_ge(prepared, i * 2 + b + 2)
                    pe.wait_ge(loaded[b], (i + 1) * (16 * nload))
                    pe.wait_ge(prepared, 1)
                pe.wait_ge(exped, i * U + n + 1)
                if packed:
                    pe.wait_ge(oready, i * U + n + 3)
                col = 0
                for cols, m in units[u].keys:
                    done = 0
                    while done < m:
                        w = min(m - done, 512 - col % 512)
                        st = cols.step or 1
                        a = cols.start + done * st
                        qs = units[u].q if isinstance(units[u].q, list) else [units[u].q]
                        for r, qc in enumerate(qs):
                            rows = slice(r * P // len(qs), (r + 1) * P // len(qs))
                            last = nc.tensor.matmul(S[rows, n % 2, col:col + w], q[:, b, qc],
                                                    k[:, b, a:a + (w - 1) * st + 1:st], start=True, stop=True)
                        col += w
                        done += w
                last.then_inc(scored, 1)

            def weigh(i, b, u):
                n = b * nu + u
                nt = len(units[u].vt)
                pe.wait_ge(exped, i * U + n + 3)
                for g in range((nt + 3) // 4):
                    G = gpos[(b, u, g)]
                    pe.wait_ge(copied[G % 2], i * ev_n[G % 2] + evs(G) + 1)
                    for t in range(4 * g, min(4 * g + 4, nt)):
                        last = nc.tensor.transpose(TR[:, G % 2, t % 4, :], pr[:, n % 2, t * P:(t + 1) * P], ident[:])
                    last.then_inc(trans, 1)
                for g in range((nt + 3) // 4):
                    G = gpos[(b, u, g)]
                    pe.wait_ge(copied[G % 2], i * ev_n[G % 2] + evs(G) + 2)
                    if g == 0:
                        pe.wait_ge(oready, i * U + n + 3)
                    for t in range(4 * g, min(4 * g + 4, nt)):
                        last = nc.tensor.matmul(O[:, n % 2, :], prT[:, n % 2, t * P:(t + 1) * P],
                                                v[:, b, units[u].vt[t], :], start=t == 0, stop=t == nt - 1)
                last.then_inc(pv, 1)

            with pe.Fori(0, heads // 2) as i:
                seq = [(b, u) for b in range(2) for u in range(nu)]
                scores(i, *seq[0])
                for n, bu in enumerate(seq):
                    if n + 1 < U:
                        scores(i, *seq[n + 1])
                    weigh(i, *bu)

        def copy_out(eng, i, b, u, par):
            nt = len(units[u].vt)
            n = b * nu + u
            for g in range((nt + 3) // 4):
                G = gpos[(b, u, g)]
                if G % 2 != par:
                    continue
                eng.wait_ge(trans, i * NG + G + 1)
                m = min(4, nt - 4 * g) * P
                dst = prT[:, n % 2, 4 * g * P:4 * g * P + m]
                src = TR[:, G % 2].rearrange("p a q -> p (a q)")[:, 0:m]
                if par == 0:
                    nc.vector.tensor_copy(dst, src).then_inc(copied[0], 1)
                else:
                    nc.scalar.activation(dst, src, ACT.Copy).then_inc(copied[1], 1)

        @block.scalar
        def _(act):
            act.sem_inc(exped, 2)
            act.sem_inc(copied[1], 1)
            with act.Fori(0, heads // 2) as i:
                for n in range(U):
                    b, u = divmod(n, nu)
                    act.wait_ge(maxed, i * U + n + 1)
                    act.wait_ge(pv, i * U + n + U - 1)
                    act.wait_ge(oready, i * U + n + 1)
                    nk = units[u].nk
                    src = sco[:, n % 2, 0:nk] if biased else S[:, n % 2, 0:nk]
                    nc.scalar.activation(pr[:, n % 2, 0:nk], src, ACT.Exp, bias=negm[:, n % 4:n % 4 + 1],
                                         scale=1.0 if biased else scale,
                                         accum_out=sums[:, n % 4:n % 4 + 1]).then_inc(exped, 1)
                    copy_out(act, i, b, u, 1)

        @block.gpsimd
        def _(pool):
            pool.sem_inc(out_free, 4)

            def landed(i, n):
                pool.wait_ge(stored[n % 2], (i * nu + n // 2 + 1) * (16 * len(out_dram(0, 0))) + before)
                pool.sem_inc(out_free, 1)

            with pool.Fori(0, heads // 2) as i:
                for b in range(2):
                    for u in range(nu):
                        n = b * nu + u
                        pool.wait_ge(oready, i * U + n + 5)
                        pool.wait_ge(oready, 1)
                        dst = out_dram(2 * i + b, u)
                        for p0, rows in dst:
                            pool.dma_start(rows, osb[p0:p0 + P // len(dst), n % 4, :]).then_inc(stored[n % 2], 16)
                        if n >= 1:
                            landed(i, n - 1)
                landed(i, U - 1)

        @block.vector
        def _(dve):
            assert U % 4 == 0
            dve.sem_inc(oready, 4)
            dve.sem_inc(copied[0], 1)
            if dk < P:
                for b in range(2):
                    nc.vector.memset(q[64 if rope is None else 96:P, b, :], 0.0)
                    nc.vector.memset(k[64 if rope is None else 96:P, b, :], 0.0)
            for view, val in bias_fill:
                for b in range(2):
                    nc.vector.memset(view(bias[:, b]), val)
            dve.drain()
            if rope is not None:
                dve.wait_ge(const_in, 16 * 8)
                nc.vector.tensor_tensor(ksw[R, :], ksw[R, :], tab[R, 1, :], ALU.mult)
                for b in range(2):
                    nc.vector.tensor_tensor(k[R, b, :], k[R, b, :], tab[R, 0, :], ALU.mult)
                dve.drain()
                for b in range(2):
                    nc.vector.tensor_tensor(k[R, b, :], k[R, b, :], ksw[R, :], ALU.add)
                dve.drain()
            dve.sem_inc(prepared, 1)

            def head_prep(i, b):
                if rope is None:
                    return
                dve.wait_ge(loaded[b], (i + 1) * (16 * nload))
                nc.vector.tensor_tensor(q[R, b, :], q[R, b, :], tab[R, 0, :], ALU.mult)
                nc.vector.tensor_tensor(qsw[R, b, :], qsw[R, b, :], tab[R, 1, :], ALU.mult)
                dve.drain()
                nc.vector.tensor_tensor(q[R, b, :], q[R, b, :], qsw[R, b, :], ALU.add).then_inc(prepared, 1)

            def finish(i, n):
                b, u = divmod(n, nu)
                dve.wait_ge(exped, i * U + n + 3)
                nc.vector.reciprocal(rinv[:, n % 4:n % 4 + 1], sums[:, n % 4:n % 4 + 1])
                dve.drain()
                dve.wait_ge(pv, i * U + n + 1 + U)
                dve.wait_ge(out_free, i * U + n + 1)
                if stats:
                    nc.vector.tensor_copy(osb[:, n % 4, dv:dv + 1], negm[:, n % 4:n % 4 + 1])
                    nc.vector.tensor_copy(osb[:, n % 4, dv + 1:dv + 2], sums[:, n % 4:n % 4 + 1])
                nc.vector.tensor_scalar(osb[:, n % 4, 0:dv], O[:, n % 2, :], rinv[:, n % 4:n % 4 + 1], None,
                                        ALU.mult).then_inc(oready, 1)

            with dve.Fori(0, heads // 2) as i:
                for n in range(U + 1):
                    if n < U:
                        b, u = divmod(n, nu)
                        nk = units[u].nk
                        if n < 2 and rope is not None:
                            head_prep(i, n)
                        if biased and u == 0:
                            dve.wait_ge(loaded[b], (i + 1) * (16 * nload))
                        dve.wait_ge(scored, i * U + n + 1)
                        if biased:
                            dve.wait_ge(exped, i * U + n + 1)
                            nc.vector.tensor_scalar(negm[:, 4:5], S[:, n % 2, 0:1], -1.0, None, ALU.mult)
                            nc.vector.tensor_tensor_reduce(
                                out=sco[:, n % 2, 0:nk], in0=S[:, n % 2, 0:nk], in1=units[u].bias(bias[:, b]),
                                scale=scale, scalar=-3.0e38, op0=ALU.add, op1=ALU.max, accum_out=negm[:, n % 4:n % 4 + 1])
                        else:
                            nc.vector.reduce_max(negm[:, n % 4:n % 4 + 1], S[:, n % 2, 0:nk], AX)
                        dve.drain()
                        nc.vector.tensor_scalar(negm[:, n % 4:n % 4 + 1], negm[:, n % 4:n % 4 + 1],
                                                -1.0 if biased else -scale, None, ALU.mult).then_inc(maxed, 1)
                    if n >= 1:
                        finish(i, n - 1)
                    if n < U:
                        copy_out(dve, i, *divmod(n, nu), 0)


def mlstm_gates(nc, name, gates_dram, bias_dram, a_dram, negm_dram, floor_dram, eps):
    with Stage(nc, name) as s:
        ig, fg, t1, t2, cs, run = (s.sb(x, [4, 2, T]) for x in ("ig", "fg", "t1", "t2", "cs", "run"))
        b = s.sb("b", [4, 4])
        in_sem, abs_sem, ln_sem, m_sem, e_sem, out_sem = (s.sem(x) for x in ("in", "biased", "logged", "maxed", "exped", "out"))
        block = s.block()

        @block.sync
        def _(sp):
            for d in range(2):
                sp.dma_start(ig[:, d, :], gates_dram[4 * d:4 * d + 4, :]).then_inc(in_sem, 16)
                sp.dma_start(fg[:, d, :], gates_dram[8 + 4 * d:12 + 4 * d, :]).then_inc(in_sem, 16)
            sp.dma_start(b[:], bias_dram).then_inc(in_sem, 16)
            sp.wait_ge(m_sem, 1)
            for d in range(2):
                sp.dma_start(a_dram[4 * d:4 * d + 4, :], ig[:, d, :]).then_inc(out_sem, 16)
                sp.dma_start(negm_dram[4 * d:4 * d + 4, :], run[:, d, :]).then_inc(out_sem, 16)
            sp.wait_ge(e_sem, 1)
            for d in range(2):
                sp.dma_start(floor_dram[4 * d:4 * d + 4, :], t2[:, d, :]).then_inc(out_sem, 16)
            sp.wait_ge(out_sem, 16 * 6)

        @block.scalar
        def _(act):
            act.wait_ge(abs_sem, 1)
            nc.scalar.activation(t1[:], fg[:], ACT.Abs)
            act.drain()
            nc.scalar.activation(t1[:], t1[:], ACT.Exp, scale=-1.0)
            act.drain()
            nc.scalar.activation(t1[:], t1[:], ACT.Ln, bias=1.0).then_inc(ln_sem, 1)
            act.wait_ge(m_sem, 1)
            nc.scalar.activation(t2[:], t2[:], ACT.Exp).then_inc(e_sem, 1)

        @block.vector
        def _(dve):
            dve.wait_ge(in_sem, 16 * 5)
            for d in range(2):
                nc.vector.tensor_scalar(ig[:, d, :], ig[:, d, :], b[:, d:d + 1], None, ALU.add)
                nc.vector.tensor_scalar(fg[:, d, :], fg[:, d, :], b[:, 2 + d:3 + d], None, ALU.add)
            dve.drain()
            dve.sem_inc(abs_sem, 1)
            dve.wait_ge(ln_sem, 1)
            nc.vector.scalar_tensor_tensor(out=fg[:], in0=fg[:], scalar=0.0, in1=t1[:], op0=ALU.min, op1=ALU.subtract)
            nc.vector.memset(t2[:], 1.0)
            dve.drain()

            def scan(dst, d0, d1, op0, op1):
                if True:
                    nc.vector.tensor_tensor_scan(dst[:, 0, :], d0[:, 0, :], d1[:, 0, :], initial=0.0, op0=op0, op1=op1)
                    nc.vector.tensor_tensor_scan(dst[:, 1, 0:NCTX][:, ::-1], d0[:, 1, 0:NCTX][:, ::-1],
                                                 d1[:, 1, 0:NCTX][:, ::-1], initial=0.0, op0=op0, op1=op1)
                    dve.drain()
                    nc.vector.tensor_tensor_scan(dst[:, 1, NCTX:T][:, ::-1], d0[:, 1, NCTX:T][:, ::-1],
                                                 d1[:, 1, NCTX:T][:, ::-1], initial=dst[:, 1, 0:1], op0=op0, op1=op1)
                    dve.drain()

            scan(cs, t2, fg, ALU.mult, ALU.add)
            nc.vector.tensor_tensor(ig[:], ig[:], cs[:], ALU.subtract)
            dve.drain()
            scan(run, ig, ig, ALU.max, ALU.max)
            nc.vector.scalar_tensor_tensor(out=t2[:], in0=cs[:], scalar=-1.0, in1=run[:], op0=ALU.mult, op1=ALU.subtract)
            dve.drain()
            nc.vector.tensor_scalar(run[:], run[:], -1.0, None, ALU.mult).then_inc(m_sem, 1)


def mlstm(nc, name, q_dram, k_dram, v_dram, conv_dram, a_dram, negm_dram, floor_dram, mask_dram, out_dram, ones):
    DH = 128
    scale = DH ** -0.5
    ops, sts = [], []
    blocks = [(0, NCTX), (NCTX, 512), (NCTX + 512, 512)]
    ends = []
    for t0, tn in blocks:
        for st in range(2 if t0 == 0 else TT):
            s0 = st * P
            for d in range(2):
                lo, hi, m = t0, t0 + tn, None
                if t0 == 0:
                    m = t0 - s0
                elif st >= 2 and d == 0:
                    if s0 >= t0 + tn:
                        continue
                    if s0 >= t0:
                        lo, m = s0, 0
                elif st >= 2:
                    if s0 + P <= t0:
                        continue
                    if s0 < t0 + tn:
                        hi, m = s0 + P, t0 - s0
                if not sts or sts[-1] != (t0, tn, st):
                    sts.append((t0, tn, st))
                ops.append((len(sts) - 1, d, lo - t0, hi - lo, m))
        ends.append(len(ops))
    last_of = {j: max(n for n, o in enumerate(ops) if o[0] == j) for j in range(len(sts))}
    masked_upto = [sum(1 for o in ops[:n] if o[4] is not None) for n in range(len(ops) + 1)]
    with nc.Fori(0, 4) as h, Stage(nc, name, turn=True) as s:
        x = s.sb("x", [P, 2, 1284])
        cv = s.sb("cv", [P, 2, T])
        qk = s.sb("qk", [P, 2, T])
        cw = s.sb("cw", [P, 2, 4])
        v = s.sb("v", [P, TT, DH])
        negm = s.sb("negm", [P, 2, T])
        floor = s.sb("floor", [P, 2, T])
        acol = s.sb("acol", [P, 2, TT])
        mask = s.sb("mask", [P, 2, 896])
        arg = s.sb("arg", [P, 2, 512])
        w = s.sb("w", [P, 4, 512])
        ws = s.sb("ws", [P, 4, 512])
        den = s.sb("den", [P, 2, 512])
        hs = s.sb("hs", [P, T])
        S = s.ps("S", [P, 2, 512])
        ND = s.ps("ND", [P, 2, 2, 512])
        x_in, in_sem, padded, conved, silued = (s.sem(c) for c in ("x_in", "in", "padded", "conved", "silued"))
        scored, argued, exped, weighed, summed, nd_free, out_sem, h_sem = (
            s.sem(c) for c in ("scored", "argued", "exped", "weighed", "summed", "nd_free", "out", "h_ready"))
        with nc.Block() as block:
            @block.sync
            def _(sp):
                for j, src in enumerate((q_dram, k_dram)):
                    sp.dma_start(x[:, j, 1:257], src[bass.ds(h * DH, DH), 0:NCTX]).then_inc(x_in, 16)
                    sp.dma_start(x[:, j, 259:1283], src[bass.ds(h * DH, DH), NCTX:T]).then_inc(x_in, 16)
                    sp.dma_start(cw[:, j, :], conv_dram[bass.ds(h * DH + j * 512, DH), :]).then_inc(x_in, 16)
                for d in range(2):
                    for dst, src in ((negm, negm_dram), (floor, floor_dram)):
                        sp.dma_start(dst[:, d, :], src[bass.ds(h + 4 * d, 1), :].broadcast_to([P, T])).then_inc(in_sem, 16)
                    sp.dma_start(acol[:, d, :], a_dram[bass.ds(h + 4 * d, 1), :].rearrange("a (j p) -> p (a j)", p=P),
                                 allow_slow_non_contiguous=True).then_inc(in_sem, 16)
                sp.dma_start(mask[:].rearrange("p a b -> p (a b)"), mask_dram).then_inc(in_sem, 16)
                sp.dma_start(v[:], v_dram.rearrange("(j p) c -> p j c", p=P)[:, :, bass.ds(h * DH, DH)]).then_inc(in_sem, 16)
                sp.wait_ge(h_sem, 1)
                sp.dma_start(out_dram[bass.ds(h * DH, DH), :], hs[:]).then_inc(out_sem, 16)
                sp.wait_ge(out_sem, 16)

            @block.scalar
            def _(act):
                for j in range(2):
                    act.wait_ge(conved, j + 1)
                    nc.scalar.activation(qk[:, j, :], cv[:, j, :], ACT.Silu).then_inc(silued, 1)
                act.wait_ge(in_sem, 16 * 8)
                for n, (j, d, c0, cn, m) in enumerate(ops):
                    t0, tn, st = sts[j]
                    if n >= 4:
                        act.wait_ge(weighed, n - 3)
                    if m is not None:
                        act.wait_ge(argued, masked_upto[n + 1])
                        nc.scalar.activation(w[:, n % 4, 0:cn], arg[:, (masked_upto[n]) % 2, 0:cn], ACT.Exp).then_inc(exped, 1)
                    else:
                        nc.scalar.activation(w[:, n % 4, 0:cn], negm[:, d, t0 + c0:t0 + c0 + cn], ACT.Exp,
                                             bias=acol[:, d, st:st + 1]).then_inc(exped, 1)

            @block.tensor
            def _(pe):
                pe.wait_ge(silued, 2)
                pe.wait_ge(in_sem, 16 * 8)

                def score(j):
                    t0, tn, st = sts[j]
                    if j >= 2:
                        pe.wait_ge(weighed, last_of[j - 2] + 1)
                    nc.tensor.matmul(S[:, j % 2, 0:tn], qk[:, 1, st * P:(st + 1) * P], qk[:, 0, t0:t0 + tn],
                                     start=True, stop=True).then_inc(scored, 1)

                score(0)
                blk = 0
                for n, (j, d, c0, cn, m) in enumerate(ops):
                    t0, tn, st = sts[j]
                    if (n == 0 or ops[n - 1][0] != j) and j + 1 < len(sts):
                        score(j + 1)
                    if n in ends[:-1]:
                        blk += 1
                        pe.wait_ge(nd_free, blk)
                    pe.wait_ge(weighed, n + 1)
                    mine = [i for i in range(0 if blk == 0 else ends[blk - 1], ends[blk]) if ops[i][1] == d]
                    for f, lhs in enumerate((v[:, st, :], ones[:])):
                        last = nc.tensor.matmul(ND[:, d, f, c0:c0 + cn], lhs, ws[:, n % 4, 0:cn],
                                                start=n == mine[0], stop=n == mine[-1])
                    last.then_inc(summed, 1)

            @block.vector
            def _(dve):
                for j in range(2):
                    for c in (0, 257, 258, 1283):
                        nc.vector.memset(x[:, j, c:c + 1], 0.0)
                dve.drain()
                dve.wait_ge(x_in, 16 * 6)
                for j in range(2):
                    for o, src, n in ((0, 0, NCTX), (NCTX, 258, NLAT)):
                        nc.vector.tensor_scalar(cv[:, j, o:o + n], x[:, j, src:src + n], cw[:, j, 0:1], cw[:, j, 3:4],
                                                ALU.mult, ALU.add)
                    for tap in (1, 2):
                        dve.drain()
                        for o, src, n in ((0, 0, NCTX), (NCTX, 258, NLAT)):
                            last = nc.vector.scalar_tensor_tensor(
                                out=cv[:, j, o:o + n], in0=x[:, j, src + tap:src + tap + n], scalar=cw[:, j, tap:tap + 1],
                                in1=cv[:, j, o:o + n], op0=ALU.mult, op1=ALU.add)
                    last.then_inc(conved, 1)
                dve.wait_ge(in_sem, 16 * 8)

                def argument(n):
                    j, d, c0, cn, m = ops[n]
                    if m is None:
                        return
                    t0, tn, st = sts[j]
                    k = masked_upto[n]
                    if k >= 2:
                        prev = max(i for i in range(n) if masked_upto[i + 1] == k - 1)
                        dve.wait_ge(exped, prev + 1)
                    nc.vector.scalar_tensor_tensor(
                        out=arg[:, k % 2, 0:cn], in0=negm[:, d, t0 + c0:t0 + c0 + cn], scalar=acol[:, d, st:st + 1],
                        in1=mask[:, d, m + 384:m + 384 + cn], op0=ALU.add, op1=ALU.min).then_inc(argued, 1)

                argument(0)
                blk = 0
                for n, (j, d, c0, cn, m) in enumerate(ops):
                    t0, tn, st = sts[j]
                    if n + 1 < len(ops):
                        argument(n + 1)
                    dve.wait_ge(exped, n + 1)
                    dve.wait_ge(scored, j + 1)
                    if n >= 4:
                        dve.wait_ge(summed, n - 3)
                    nc.vector.scalar_tensor_tensor(
                        out=ws[:, n % 4, 0:cn], in0=S[:, j % 2, c0:c0 + cn], scalar=scale, in1=w[:, n % 4, 0:cn],
                        op0=ALU.mult, op1=ALU.mult).then_inc(weighed, 1)
                    if n + 1 == ends[blk]:
                        dve.wait_ge(summed, n + 1)
                        for d2 in range(2):
                            nc.vector.scalar_tensor_tensor(out=den[:, d2, 0:tn], in0=ND[:, d2, 1, 0:tn], scalar=-1.0,
                                                           in1=floor[:, d2, t0:t0 + tn], op0=ALU.mult, op1=ALU.max)
                        dve.drain()
                        for d2 in range(2):
                            nc.vector.tensor_tensor(den[:, d2, 0:tn], ND[:, d2, 1, 0:tn], den[:, d2, 0:tn], ALU.max)
                        dve.drain()
                        nc.vector.reciprocal(den[:, :, 0:tn], den[:, :, 0:tn])
                        dve.drain()
                        nc.vector.tensor_tensor(hs[:, t0:t0 + tn], ND[:, 0, 0, 0:tn], den[:, 0, 0:tn], ALU.mult)
                        nc.vector.tensor_tensor(den[:, 1, 0:tn], ND[:, 1, 0, 0:tn], den[:, 1, 0:tn], ALU.mult)
                        dve.drain()
                        last = nc.vector.tensor_tensor(hs[:, t0:t0 + tn], hs[:, t0:t0 + tn], den[:, 1, 0:tn], ALU.add)
                        last.then_inc(nd_free, 1)
                        blk += 1
                        if blk == 3:
                            dve.drain()
                            dve.sem_inc(h_sem, 1)
        s.reset()


def mlstm_masks():
    p = np.arange(P)[:, None]
    x = np.arange(896)[None, :] - 384
    return np.concatenate([np.where(x >= p, 0.0, NEG), np.where(x <= p, 0.0, NEG)], 1).astype(np.float32)


def gla(nc, name, q_dram, k_dram, v_dram, ga_dram, wg_dram, bg_dram, reset_dram, clamp_dram, mask_dram, out_dram, ident):
    NI = 8
    with nc.Fori(0, 2) as hp, Stage(nc, name, turn=True) as s:
        q, k, = s.sb("q", [P, T]), s.sb("k", [P, T])
        v = s.sb("v", [P, TT, 256])
        ga = s.sb("ga", [16, 2, T])
        wg = s.sb("wg", [16, 2, P])
        bg = s.sb("bg", [P, 2])
        keep = s.sb("keep", [P, 2, T])
        clamp = s.sb("clamp", [P, NI, P])
        mask = s.sb("mask", [P, 2, NI, 2, 16])
        t1, t2 = s.sb("t1", [P, T]), s.sb("t2", [P, T])
        b = s.sb("b", [P, 2, T])
        q2, q2s = s.sb("q2", [P, 2, T]), s.sb("q2s", [P, 2, T])
        arg = s.sb("arg", [P, 2, NI, P])
        ks = s.sb("ks", [P, 2, NI, P])
        kd = s.sb("kd", [P, 2, P])
        kdT = s.sb("kdT", [P, 2, P])
        att = s.sb("att", [P, 2, 2, P])
        dl = s.sb("dl", [P, 2])
        S = s.sb("S", [P, P])
        osum = s.sb("osum", [P, 2, NLAT])
        G = s.ps("G", [P, 3 * 512])
        A = s.ps("A", [P, 2, 512])
        TR, O, UP = s.ps("TR", [P, 512]), s.ps("O", [P, 512]), s.ps("UP", [P, 512])
        in_sem, zeroed, gated, absed, logged, cum, qexp, qmul = (
            s.sem(c) for c in ("in", "zeroed", "gated", "absed", "logged", "cum", "qexp", "qmul"))
        argd, kexp, dexp, ksd, kdd, scored, tr_done, tr_copied, att_sem, up_done, s_sem, out_sem = (
            s.sem(c) for c in ("argd", "kexp", "dexp", "ks_ready", "kd_ready", "scored", "tr_done", "tr_copied",
                               "att_ready", "up_done", "state", "out"))
        orders = [list(range(TT)), [1, 0] + list(range(TT - 1, 1, -1))]
        seq = [(d, c) for d in range(2) for c in orders[d]]
        lat = [c >= 2 for _, c in seq]
        nlat = [sum(lat[:n]) for n in range(len(seq) + 1)]
        N = len(seq)
        with nc.Block() as block:
            @block.sync
            def _(sp):
                sp.dma_start(q[:], q_dram[bass.ds(hp * P, P), :]).then_inc(in_sem, 16)
                sp.dma_start(k[:], k_dram[bass.ds(hp * P, P), :]).then_inc(in_sem, 16)
                sp.dma_start(v[:], v_dram.rearrange("(j p) c -> p j c", p=P)[:, :, bass.ds(hp * 256, 256)]).then_inc(in_sem, 16)
                for d in range(2):
                    sp.dma_start(ga[:, d, :], ga_dram[16 * d:16 * d + 16, :]).then_inc(in_sem, 16)
                    sp.dma_start(wg[:, d, :], wg_dram[16 * d:16 * d + 16, bass.ds(hp * P, P)]).then_inc(in_sem, 16)
                sp.dma_start(bg[:], bg_dram[bass.ds(hp * P, P), :]).then_inc(in_sem, 16)
                sp.dma_start(keep[:].rearrange("p a t -> p (a t)"), reset_dram).then_inc(in_sem, 16)
                sp.dma_start(clamp[:].rearrange("p a t -> p (a t)"), clamp_dram).then_inc(in_sem, 16)
                sp.dma_start(mask[:].rearrange("p a i h t -> p (a i h t)"), mask_dram).then_inc(in_sem, 16)
                sp.wait_ge(s_sem, N)
                for h in range(2):
                    sp.dma_start(out_dram[bass.ds(hp * 256 + h * P, P), :], osum[:, h, :]).then_inc(out_sem, 16)
                sp.wait_ge(out_sem, 32)

            @block.tensor
            def _(pe):
                pe.wait_ge(in_sem, 16 * 11)
                for d in range(2):
                    if d:
                        pe.wait_ge(cum, 1)
                    for o, n in chunks(0, T):
                        last = nc.tensor.matmul(G[:, o:o + n], wg[:, d, :], ga[:, d, o:o + n], start=True, stop=True)
                    last.then_inc(gated, 1)

                def first(n):
                    d, c = seq[n]
                    if lat[n]:
                        if nlat[n] >= 2:
                            pe.wait_ge(att_sem, nlat[n] - 1)
                        pe.wait_ge(ksd, nlat[n] + 1)
                        if c == orders[d][2]:
                            pe.wait_ge(qmul, 2 * d + 1)
                        for i in range(NI):
                            t = c * P + 16 * i
                            last = nc.tensor.matmul(A[:, nlat[n] % 2, 32 * i:32 * i + 32], ks[:, nlat[n] % 2, i, :],
                                                    q2[:, :, t:t + 16], start=True, stop=True)
                        last.then_inc(scored, 1)
                    pe.wait_ge(kdd, n + 1)
                    if n >= 1:
                        pe.wait_ge(tr_copied, n)
                    nc.tensor.transpose(TR[:, 0:P], kd[:, n % 2, :], ident[:]).then_inc(tr_done, 1)

                first(0)
                for n, (d, c) in enumerate(seq):
                    pe.wait_ge(tr_copied, n + 1)
                    if n >= 1:
                        pe.wait_ge(s_sem, n)
                    if lat[n]:
                        pe.wait_ge(att_sem, nlat[n + 1])
                        for h in range(2):
                            nc.tensor.matmul(O[:, h * P:(h + 1) * P], v[:, c, h * P:(h + 1) * P],
                                             att[:, nlat[n] % 2, h, :], start=True, stop=False)
                            nc.tensor.matmul(O[:, h * P:(h + 1) * P], S[:], q2s[:, h, c * P:(c + 1) * P],
                                             start=False, stop=True)
                    nc.tensor.matmul(UP[:, 0:256], kdT[:, n % 2, :], v[:, c, :], start=True, stop=True).then_inc(up_done, 1)
                    if n + 1 < N:
                        first(n + 1)

            @block.scalar
            def _(act):
                act.wait_ge(in_sem, 16 * 11)
                for d in range(2):
                    act.wait_ge(gated, d + 1)
                    nc.scalar.activation(t1[:], G[:, 0:T], ACT.Abs, bias=bg[:, d:d + 1]).then_inc(absed, 1)
                    act.drain()
                    nc.scalar.activation(t1[:], t1[:], ACT.Exp, scale=-1.0)
                    act.drain()
                    nc.scalar.activation(t1[:], t1[:], ACT.Ln, bias=1.0).then_inc(logged, 1)
                    act.wait_ge(cum, d + 1)
                def decays(n):
                    d, c = seq[n]
                    if c == orders[d][0]:
                        act.wait_ge(qexp, 2 * d + 1)
                        nc.scalar.activation(t1[:], t1[:], ACT.Exp)
                        nc.scalar.activation(t2[:], b[:, d, :], ACT.Exp).then_inc(qexp, 1)
                    last = c * P + (P - 1 if d == 0 else 0)
                    if n >= 2:
                        act.wait_ge(tr_done, n - 1)
                    nc.scalar.activation(kd[:, n % 2, :], b[:, d, c * P:(c + 1) * P], ACT.Exp, bias=b[:, d, last:last + 1], scale=-1.0)
                    if n >= 2:
                        act.wait_ge(s_sem, n - 1)
                    nc.scalar.activation(dl[:, n % 2:n % 2 + 1], b[:, d, last:last + 1], ACT.Exp).then_inc(dexp, 1)
                    if lat[n]:
                        act.wait_ge(argd, nlat[n + 1])
                        if nlat[n] >= 2:
                            act.wait_ge(scored, nlat[n] - 1)
                        nc.scalar.activation(ks[:, nlat[n] % 2], arg[:, nlat[n] % 2], ACT.Exp).then_inc(kexp, 1)

                decays(0)
                for n, (d, c) in enumerate(seq):
                    ahead = n + 1 < N and seq[n + 1][0] == d
                    if ahead:
                        decays(n + 1)
                    act.wait_ge(tr_done, n + 1)
                    if n >= 2:
                        act.wait_ge(up_done, n - 1)
                    nc.scalar.activation(kdT[:, n % 2, :], TR[:, 0:P], ACT.Copy).then_inc(tr_copied, 1)
                    if n + 1 < N and not ahead:
                        decays(n + 1)

            @block.vector
            def _(dve):
                nc.vector.memset(q2[:], 0.0)
                nc.vector.memset(q2s[:], 0.0)
                dve.wait_ge(in_sem, 16 * 11)
                for d in range(2):
                    dve.wait_ge(absed, d + 1)
                    nc.vector.tensor_scalar(t2[:], G[:, 0:T], bg[:, d:d + 1], 0.0, ALU.add, ALU.min)
                    dve.drain()
                    dve.wait_ge(logged, d + 1)
                    nc.vector.tensor_tensor(t2[:], t2[:], t1[:], ALU.subtract)
                    dve.drain()
                    nc.vector.tensor_scalar(t2[:], t2[:], 1.0 / 16.0, None, ALU.mult)
                    dve.drain()
                    f = (lambda a: a[:, ::-1]) if d else (lambda a: a)
                    nc.vector.tensor_tensor_scan(f(b[:, d, :]), f(keep[:, d, :]), f(t2[:]), initial=0.0,
                                                 op0=ALU.mult, op1=ALU.add).then_inc(cum, 1)
                    dve.drain()

                def queries(d):
                    if d:
                        dve.wait_ge(up_done, TT)
                    bb = b[:, d, :].rearrange("p (i t) -> p i t", t=16)
                    nc.vector.tensor_tensor(t1[:].rearrange("p (i t) -> p i t", t=16), bb,
                                            bb[:, :, 8:9].broadcast_to([P, T // 16, 16]), ALU.subtract)
                    dve.drain()
                    nc.vector.tensor_scalar(t1[:], t1[:], 85.0, None, ALU.min).then_inc(qexp, 1)
                    dve.wait_ge(qexp, 2 * d + 2)
                    for h in range(2):
                        r = slice(64 * h, 64 * h + 64)
                        for dst, e in ((q2, t1), (q2s, t2)):
                            last = nc.vector.scalar_tensor_tensor(out=dst[r, h, :], in0=q[r, :], scalar=64 ** -0.5,
                                                                  in1=e[r, :], op0=ALU.mult, op1=ALU.mult)
                    last.then_inc(qmul, 1)
                    nc.vector.memset(S[:], 0.0).then_inc(qmul, 1)
                    dve.drain()

                def exponents(n):
                    d, c = seq[n]
                    if not lat[n]:
                        return
                    a = arg[:, nlat[n] % 2]
                    bc = b[:, d, c * P:(c + 1) * P]
                    if nlat[n] >= 2:
                        dve.wait_ge(kexp, nlat[n] - 1)
                    nc.vector.tensor_tensor(a, bc.rearrange("p (i t) -> p i t", t=16)[:, :, 8:9].broadcast_to([P, NI, P]),
                                            bc.rearrange("p (o t) -> p o t", o=1).broadcast_to([P, NI, P]), ALU.subtract)
                    dve.drain()
                    nc.vector.tensor_tensor(a, a, clamp[:], ALU.min).then_inc(argd, 1)

                def keys(n):
                    d, c = seq[n]
                    kc = k[:, c * P:(c + 1) * P]
                    dve.wait_ge(dexp, n + 1)
                    nc.vector.tensor_tensor(kd[:, n % 2, :], kd[:, n % 2, :], kc, ALU.mult).then_inc(kdd, 1)
                    if lat[n]:
                        dve.wait_ge(kexp, nlat[n + 1])
                        kk = ks[:, nlat[n] % 2]
                        nc.vector.tensor_tensor(kk, kk, kc.rearrange("p (o t) -> p o t", o=1).broadcast_to([P, NI, P]),
                                                ALU.mult).then_inc(ksd, 1)

                def weights(n):
                    if not lat[n]:
                        return
                    d, c = seq[n]
                    dve.wait_ge(scored, nlat[n + 1])
                    if nlat[n] >= 2:
                        dve.wait_ge(up_done, n - 1)
                    nc.vector.tensor_tensor(att[:, nlat[n] % 2].rearrange("p h (i t) -> p i h t", t=16),
                                            A[:, nlat[n] % 2, 0:256].rearrange("p (i h t) -> p i h t", h=2, t=16),
                                            mask[:, d], ALU.mult).then_inc(att_sem, 1)

                def state(n):
                    d, c = seq[n]
                    dve.wait_ge(up_done, n + 1)
                    if lat[n]:
                        dst = osum[:, :, (c - 2) * P:(c - 1) * P]
                        src = O[:, 0:256].rearrange("p (h t) -> p h t", h=2)
                        if d == 0:
                            nc.vector.tensor_copy(dst, src)
                        else:
                            nc.vector.tensor_tensor(dst, dst, src, ALU.add)
                    for h in range(2):
                        r = slice(64 * h, 64 * h + 64)
                        nc.vector.scalar_tensor_tensor(out=S[r, :], in0=S[r, :], scalar=dl[r, n % 2:n % 2 + 1],
                                                       in1=UP[r, h * P:(h + 1) * P], op0=ALU.mult, op1=ALU.add)
                    dve.drain()
                    dve.sem_inc(s_sem, 1)

                queries(0)
                exponents(0)
                keys(0)
                for n, (d, c) in enumerate(seq):
                    if n + 1 < N and seq[n + 1][0] == d:
                        exponents(n + 1)
                        weights(n)
                        keys(n + 1)
                        state(n)
                    else:
                        weights(n)
                        state(n)
                        if n + 1 < N:
                            queries(d + 1)
                            exponents(n + 1)
                            keys(n + 1)
        s.reset()


def gla_consts():
    t = np.arange(T)
    keep = np.stack([t % P != 0, t % P != P - 1]).astype(np.float32)
    i, sx, tt = np.arange(8), np.arange(P), np.arange(16)
    clamp = np.where(sx[None, :] // 16 == i[:, None], 85.0, 0.0).astype(np.float32)
    pos = i[:, None] * 16 + tt[None, :]
    m = np.stack([sx[:, None, None] <= pos, sx[:, None, None] >= pos], 1)
    m = np.broadcast_to(m[:, :, :, None, :], (P, 2, 8, 2, 16)).astype(np.float32)
    one = np.ones((P, 1), np.float32)
    return one * keep.reshape(1, -1), one * clamp.reshape(1, -1), np.ascontiguousarray(m).reshape(P, -1)


def gated_mix(nc, name, tm_dram, tm_at, fm_dram, fm_at, mo_dram, z_dram, g_dram, t0, tn, fm_cols, y, ident, ones, eps):
    nt = tn // P
    parts = chunks(0, tn)
    with Stage(nc, name) as s:
        a = s.sb("a", [P, nt, 512])
        z = s.sb("z", [P, 2, tn])
        h = s.sb("h", [P, tn])
        mo = s.sb("mo", [P, tn])
        sq = s.sb("sq", [P, tn])
        g = s.sb("g", [P, 4])
        TR = s.ps("TR", [P, 2, 512])
        SS = s.ps("SS", [P, 3 * 512])
        a_in, used = s.sem("a_in"), s.sem("used")
        z_in = [s.sem(f"z_in{b}") for b in range(2)]
        silued, tr_done, tr_used = s.sem("silued"), s.sem("tr_done"), s.sem("tr_used")
        h_in, sig, gated, squared, summed, rooted = (s.sem(x) for x in ("h_in", "sig", "gated", "squared", "summed", "rooted"))
        block = s.block()
        order = [("t", j) for j in range(4)] + [("f", j) for j in range(4)]
        zrow = [(tm_at if kind == "t" else fm_at) + j for kind, j in order]
        nh = 3 if mo_dram is None else 4
        nh = 1 + (mo_dram is not None)

        @block.sync
        def _(sp):
            sp.dma_start(a[:], tm_dram.rearrange("(t p) c -> p t c", p=P)).then_inc(a_in, 16)
            sp.dma_start(g[:], g_dram).then_inc(a_in, 16)
            for n, (kind, j) in enumerate(order):
                if n >= 2:
                    sp.wait_ge(used, n - 1)
                r = zrow[n] * P
                sp.dma_start(z[:, n % 2, :], z_dram[r:r + P, t0:t0 + tn]).then_inc(z_in[n % 2], 16)
                if kind == "f":
                    sp.wait_ge(used, n)
                    sp.dma_start(h[:], fm_dram[j * P:(j + 1) * P, fm_cols:fm_cols + tn]).then_inc(h_in, 16)
                    if mo_dram is not None:
                        sp.dma_start(mo[:], mo_dram[j * P:(j + 1) * P, t0:t0 + tn]).then_inc(h_in, 16)

        @block.scalar
        def _(act):
            for n, (kind, j) in enumerate(order):
                act.wait_ge(z_in[n % 2], 16 * (n // 2 + 1))
                nc.scalar.activation(z[:, n % 2, :], z[:, n % 2, :], ACT.Silu).then_inc(silued, 1)
                if kind == "f":
                    act.wait_ge(h_in, 16 * nh * (j + 1))
                    if mo_dram is not None:
                        nc.scalar.activation(mo[:], mo[:], ACT.Sigmoid).then_inc(sig, 1)
                        act.wait_ge(gated, j + 1)
                    nc.scalar.activation(sq[:], h[:], ACT.Square).then_inc(squared, 1)
                    act.wait_ge(summed, j + 1)
                    nc.scalar.activation(sq[:], SS[:, 0:tn], ACT.Sqrt, bias=eps, scale=1.0 / P).then_inc(rooted, 1)

        @block.tensor
        def _(pe):
            pe.wait_ge(a_in, 32)
            m = 0
            for j in range(4):
                for o, n in parts:
                    if m >= 2:
                        pe.wait_ge(tr_used, m - 1)
                    for t in range(n // P):
                        last = nc.tensor.transpose(TR[:, m % 2, t * P:(t + 1) * P],
                                                   a[:, o // P + t, j * P:(j + 1) * P], ident[:])
                    last.then_inc(tr_done, 1)
                    m += 1
            for j in range(4):
                pe.wait_ge(squared, j + 1)
                for o, n in parts:
                    last = nc.tensor.matmul(SS[:, o:o + n], ones[:], sq[:, o:o + n], start=True, stop=True)
                last.then_inc(summed, 1)

        @block.vector
        def _(dve):
            dve.wait_ge(a_in, 32)
            m = 0
            for n, (kind, j) in enumerate(order):
                k = zrow[n]
                if kind == "t":
                    dve.wait_ge(silued, n + 1)
                    for o, w in parts:
                        dve.wait_ge(tr_done, m + 1)
                        nc.vector.tensor_tensor(y[:, k, t0 + o:t0 + o + w], TR[:, m % 2, 0:w], z[:, n % 2, o:o + w],
                                                ALU.mult).then_inc(tr_used, 1)
                        m += 1
                    dve.drain()
                    dve.sem_inc(used, 1)
                    continue
                if mo_dram is not None:
                    dve.wait_ge(sig, j + 1)
                    nc.vector.tensor_tensor(h[:], h[:], mo[:], ALU.mult).then_inc(gated, 1)
                dve.wait_ge(rooted, j + 1)
                nc.vector.reciprocal(sq[:], sq[:])
                dve.drain()
                nc.vector.scalar_tensor_tensor(out=h[:], in0=h[:], scalar=g[:, j:j + 1], in1=sq[:], op0=ALU.mult, op1=ALU.mult)
                dve.drain()
                nc.vector.tensor_tensor(y[:, k, t0:t0 + tn], h[:], z[:, n % 2, :], ALU.mult).then_inc(used, 1)


def to_features(nc, name, tm_dram, nt, width, y, ident):
    with Stage(nc, name) as s:
        a = s.sb("a", [P, nt, width])
        TR = s.ps("TR", [P, 2, 512])
        a_in, done, used = s.sem("a_in"), s.sem("done"), s.sem("used")
        block = s.block()
        tiles = [(j, o, n) for j in range(width // P) for o, n in chunks(0, nt * P)]

        @block.sync
        def _(sp):
            sp.dma_start(a[:], tm_dram.rearrange("(t p) c -> p t c", p=P)).then_inc(a_in, 16)

        @block.tensor
        def _(pe):
            pe.wait_ge(a_in, 16)
            for m, (j, o, n) in enumerate(tiles):
                if m >= 2:
                    pe.wait_ge(used, m - 1)
                for t in range(n // P):
                    last = nc.tensor.transpose(TR[:, m % 2, t * P:(t + 1) * P], a[:, o // P + t, j * P:(j + 1) * P], ident[:])
                last.then_inc(done, 1)

        @block.vector
        def _(dve):
            for m, (j, o, n) in enumerate(tiles):
                dve.wait_ge(done, m + 1)
                nc.vector.tensor_copy(y[:, j, o:o + n], TR[:, m % 2, 0:n]).then_inc(used, 1)


def table_rows(nc, name, lhs_dram, hot_dram, kk, m, n, out_dram, mul):
    with Stage(nc, name) as s:
        lhs, hot, res = s.sb("lhs", [kk, m]), s.sb("hot", [kk, n]), s.sb("res", [m, n])
        acc = s.ps("acc", [P, 2, 512])
        l_in, mm, cp, st = s.sem("in"), s.sem("mm"), s.sem("copied"), s.sem("stored")
        block = s.block()
        parts = chunks(0, n)

        @block.sync
        def _(sp):
            sp.dma_start(lhs[:], lhs_dram).then_inc(l_in, 16)
            sp.dma_start(hot[:], hot_dram).then_inc(l_in, 16)
            sp.wait_ge(cp, len(parts))
            sp.dma_start(out_dram, res[:]).then_inc(st, 16)
            sp.wait_ge(st, 16)

        @block.tensor
        def _(pe):
            pe.wait_ge(l_in, 32)
            for c, (o, w) in enumerate(parts):
                if c >= 2:
                    pe.wait_ge(cp, c - 1)
                nc.tensor.matmul(acc[0:m, c % 2, 0:w], lhs[:], hot[:, o:o + w], start=True, stop=True).then_inc(mm, 1)

        @block.vector
        def _(dve):
            for c, (o, w) in enumerate(parts):
                dve.wait_ge(mm, c + 1)
                nc.vector.tensor_scalar(res[:, o:o + w], acc[0:m, c % 2, 0:w], mul, None, ALU.mult).then_inc(cp, 1)


def softplus_column(nc, name, lam_dram, n, out):
    with Stage(nc, name) as s:
        lam, e, z, z2, acc = (s.sb(c, [P, n]) for c in ("lam", "e", "z", "z2", "acc"))
        l_in, ex = s.sem("in"), s.sem("exped")
        block = s.block()

        @block.sync
        def _(sp):
            sp.dma_start(lam[:], lam_dram).then_inc(l_in, 16)

        @block.scalar
        def _(act):
            act.wait_ge(l_in, 16)
            nc.scalar.activation(e[:], lam[:], ACT.Abs)
            act.drain()
            nc.scalar.activation(e[:], e[:], ACT.Exp, scale=-1.0).then_inc(ex, 1)

        @block.vector
        def _(dve):
            dve.wait_ge(ex, 1)
            nc.vector.tensor_scalar(z[:], e[:], 2.0, None, ALU.add)
            dve.drain()
            nc.vector.reciprocal(z[:], z[:])
            dve.drain()
            nc.vector.tensor_tensor(z[:], z[:], e[:], ALU.mult)
            dve.drain()
            nc.vector.tensor_tensor(z2[:], z[:], z[:], ALU.mult)
            nc.vector.memset(acc[:], 1.0 / 19)
            dve.drain()
            for p in range(17, 0, -2):
                nc.vector.tensor_tensor(acc[:], acc[:], z2[:], ALU.mult)
                dve.drain()
                nc.vector.tensor_scalar(acc[:], acc[:], 1.0 / p, None, ALU.add)
                dve.drain()
            nc.vector.tensor_tensor(acc[:], acc[:], z[:], ALU.mult)
            nc.vector.tensor_scalar(lam[:], lam[:], -1.0, 0.0, ALU.mult, ALU.max)
            dve.drain()
            nc.vector.scalar_tensor_tensor(out=out[:], in0=acc[:], scalar=2.0, in1=lam[:], op0=ALU.mult, op1=ALU.add)


def rg_lru(nc, name, x_dram, gate_dram, par_dram, wa_dram, wx_dram, sp_dram, out_dram):
    with nc.Fori(0, 6) as i, Stage(nc, name, turn=True) as s:
        x = s.sb("x", [P, 3 + NLAT])
        gt = s.sb("gt", [P, NLAT])
        par = s.sb("par", [P, 8])
        spc = s.sb("spc", [P, 4])
        wa, wx = s.sb("wa", [P, P]), s.sb("wx", [P, P])
        xc, r, ig, av, tn, h, g1 = (s.sb(c, [P, NLAT]) for c in ("xc", "r", "ig", "av", "tn", "h", "g1"))
        R = s.ps("R", [P, 2, NLAT])
        in_sem, conv, mm, sig, ax, m2, root, gel, gs, h_sem, out_sem, sc = (
            s.sem(c) for c in ("in", "conved", "mm", "sig", "ax", "m2", "root", "gel", "gs", "h_ready", "out", "scales"))
        with nc.Block() as block:
            @block.sync
            def _(sp):
                rows = bass.ds(i * P, P)
                for dst, src in ((x[:, 3:3 + NLAT], x_dram), (gt[:], gate_dram), (par[:], par_dram), (wa[:], wa_dram),
                                 (wx[:], wx_dram), (spc[:, 0:1], sp_dram)):
                    sp.dma_start(dst, src[rows, :]).then_inc(in_sem, 16)
                sp.wait_ge(h_sem, 1)
                sp.dma_start(out_dram[rows, :], h[:]).then_inc(out_sem, 16)
                sp.wait_ge(out_sem, 16)

            @block.tensor
            def _(pe):
                pe.wait_ge(in_sem, 96)
                pe.wait_ge(conv, 1)
                for j, wt in enumerate((wa, wx)):
                    for o in (0, 512):
                        last = nc.tensor.matmul(R[:, j, o:o + 512], wt[:], xc[:, o:o + 512], start=True, stop=True)
                last.then_inc(mm, 1)

            @block.scalar
            def _(act):
                act.wait_ge(mm, 1)
                nc.scalar.activation(r[:], R[:, 0, :], ACT.Sigmoid, bias=par[:, 5:6])
                nc.scalar.activation(ig[:], R[:, 1, :], ACT.Sigmoid, bias=par[:, 6:7]).then_inc(sig, 1)
                act.wait_ge(gel, 1)
                nc.scalar.activation(g1[:], g1[:], ACT.Sigmoid, scale=1.5957691216057308).then_inc(gs, 1)
                act.wait_ge(sc, 1)
                act.drain()
                nc.scalar.activation(av[:], r[:], ACT.Exp, scale=spc[:, 1:2])
                nc.scalar.activation(tn[:], r[:], ACT.Tanh, scale=spc[:, 2:3]).then_inc(ax, 1)
                act.wait_ge(m2, 1)
                nc.scalar.activation(tn[:], tn[:], ACT.Sqrt).then_inc(root, 1)

            @block.vector
            def _(dve):
                nc.vector.memset(x[:, 0:3], 0.0)
                dve.drain()
                dve.wait_ge(in_sem, 96)
                nc.vector.tensor_scalar(spc[:, 1:2], spc[:, 0:1], -8.0, None, ALU.mult)
                nc.vector.tensor_scalar(spc[:, 2:3], spc[:, 0:1], 8.0, None, ALU.mult).then_inc(sc, 1)
                nc.vector.tensor_scalar(xc[:], x[:, 0:NLAT], par[:, 0:1], par[:, 4:5], ALU.mult, ALU.add)
                for tap in (1, 2, 3):
                    dve.drain()
                    last = nc.vector.scalar_tensor_tensor(out=xc[:], in0=x[:, tap:tap + NLAT], scalar=par[:, tap:tap + 1],
                                                          in1=xc[:], op0=ALU.mult, op1=ALU.add)
                last.then_inc(conv, 1)
                nc.vector.tensor_tensor(g1[:], gt[:], gt[:], ALU.mult)
                dve.drain()
                nc.vector.tensor_scalar(g1[:], g1[:], 0.044715, 1.0, ALU.mult, ALU.add)
                dve.drain()
                nc.vector.tensor_tensor(g1[:], g1[:], gt[:], ALU.mult).then_inc(gel, 1)
                dve.wait_ge(gs, 1)
                nc.vector.tensor_tensor(gt[:], gt[:], g1[:], ALU.mult)
                dve.wait_ge(sig, 1)
                nc.vector.tensor_tensor(ig[:], ig[:], xc[:], ALU.mult)
                dve.wait_ge(ax, 1)
                dve.drain()
                nc.vector.tensor_tensor(g1[:], av[:], av[:], ALU.mult)
                dve.drain()
                nc.vector.scalar_tensor_tensor(out=tn[:], in0=g1[:], scalar=1.0, in1=tn[:], op0=ALU.add, op1=ALU.mult).then_inc(m2, 1)
                dve.wait_ge(root, 1)
                nc.vector.tensor_tensor(ig[:], ig[:], tn[:], ALU.mult)
                dve.drain()
                nc.vector.tensor_tensor_scan(h[:], av[:], ig[:], initial=0.0, op0=ALU.mult, op1=ALU.add)
                dve.drain()
                nc.vector.tensor_tensor(h[:], h[:], gt[:], ALU.mult).then_inc(h_sem, 1)
        s.reset()


def combine_groups(nc, name, o_dram, out_dram):
    with Stage(nc, name) as s:
        o = s.sb("o", [P, 8, 12, 66])
        low, w, tot = s.sb("low", [P, 8, 4]), s.sb("w", [P, 8, 12]), s.sb("tot", [P, 8, 4])
        res = s.sb("res", [P, 8, 4, 64])
        l_in, sub, ex, rs, st = (s.sem(c) for c in ("in", "sub", "exped", "res", "stored"))
        block = s.block()

        @block.sync
        def _(sp):
            sp.dma_start(o[:].rearrange("p t h c -> p t (h c)"), o_dram.rearrange("(t p) c -> p t c", p=P)).then_inc(l_in, 16)
            sp.wait_ge(rs, 1)
            sp.dma_start(out_dram.rearrange("(t p) c -> p t c", p=P), res[:].rearrange("p t h c -> p t (h c)")).then_inc(st, 16)
            sp.wait_ge(st, 16)

        @block.scalar
        def _(act):
            act.wait_ge(sub, 1)
            nc.scalar.activation(w[:], w[:], ACT.Exp).then_inc(ex, 1)

        @block.vector
        def _(dve):
            dve.wait_ge(l_in, 16)
            nm = [o[:, :, 4 * g:4 * g + 4, 64] for g in range(3)]
            nc.vector.tensor_tensor(low[:], nm[0], nm[1], ALU.min)
            dve.drain()
            nc.vector.tensor_tensor(low[:], low[:], nm[2], ALU.min)
            dve.drain()
            for g in range(3):
                nc.vector.tensor_tensor(w[:, :, 4 * g:4 * g + 4], low[:], nm[g], ALU.subtract)
            dve.drain()
            dve.sem_inc(sub, 1)
            dve.wait_ge(ex, 1)
            nc.vector.tensor_tensor(w[:], w[:], o[:, :, :, 65], ALU.mult)
            dve.drain()
            nc.vector.tensor_tensor(tot[:], w[:, :, 0:4], w[:, :, 4:8], ALU.add)
            dve.drain()
            nc.vector.tensor_tensor(tot[:], tot[:], w[:, :, 8:12], ALU.add)
            dve.drain()
            nc.vector.reciprocal(tot[:], tot[:])
            dve.drain()
            for t in range(8):
                for g in range(3):
                    for h in range(4):
                        c = 4 * g + h
                        if g == 0:
                            nc.vector.tensor_scalar(res[:, t, h, :], o[:, t, c, 0:64], w[:, t, c:c + 1], None, ALU.mult)
                        else:
                            nc.vector.scalar_tensor_tensor(out=res[:, t, h, :], in0=o[:, t, c, 0:64], scalar=w[:, t, c:c + 1],
                                                           in1=res[:, t, h, :], op0=ALU.mult, op1=ALU.add)
                    dve.drain()
                for h in range(4):
                    last = nc.vector.tensor_scalar(res[:, t, h, :], res[:, t, h, :], tot[:, t, h:h + 1], None, ALU.mult)
            dve.drain()
            dve.sem_inc(rs, 1)


def merge_branches(nc, name, gates_dram, b_dram, y_dram, out):
    with Stage(nc, name) as s:
        g, y = s.sb("g", [P, 2, 3, NLAT]), s.sb("y", [P, 2, 3, NLAT])
        b = s.sb("b", [P, 3 * KD])
        b_in, sig, used = s.sem("b_in"), s.sem("sig"), s.sem("used")
        t_in = [s.sem(f"in{k}") for k in range(2)]
        block = s.block()

        @block.sync
        def _(sp):
            sp.dma_start(b[:], b_dram).then_inc(b_in, 16)
            gv = gates_dram.rearrange("(b j p) t -> j p b t", b=3, p=P)
            yv = y_dram.rearrange("(b j p) t -> j p b t", b=3, p=P)
            for j in range(KD):
                if j >= 2:
                    sp.wait_ge(used, j - 1)
                sp.dma_start(g[:, j % 2], gv[j]).then_inc(t_in[j % 2], 16)
                sp.dma_start(y[:, j % 2], yv[j]).then_inc(t_in[j % 2], 16)

        @block.scalar
        def _(act):
            act.wait_ge(b_in, 16)
            for j in range(KD):
                act.wait_ge(t_in[j % 2], 32 * (j // 2 + 1))
                for k in range(3):
                    last = nc.scalar.activation(g[:, j % 2, k, :], g[:, j % 2, k, :], ACT.Sigmoid,
                                                bias=b[:, k * KD + j:k * KD + j + 1])
                last.then_inc(sig, 1)

        @block.vector
        def _(dve):
            for j in range(KD):
                dve.wait_ge(sig, j + 1)
                nc.vector.tensor_tensor(g[:, j % 2], g[:, j % 2], y[:, j % 2], ALU.mult)
                dve.drain()
                nc.vector.tensor_tensor(g[:, j % 2, 0, :], g[:, j % 2, 0, :], g[:, j % 2, 1, :], ALU.add)
                dve.drain()
                nc.vector.tensor_tensor(out[:, j, NCTX:T], g[:, j % 2, 0, :], g[:, j % 2, 2, :], ALU.add).then_inc(used, 1)


def load(nc, name, pairs):
    with Stage(nc, name) as s:
        done = s.sem("done")
        block = s.block()

        @block.sync
        def _(sp):
            for dst, src in pairs:
                sp.dma_start(dst, src).then_inc(done, 16)
            sp.wait_ge(done, 16 * len(pairs))

CQ, CKV, KR, GT, MQ, MK, MO, Z0 = 0, 384, 640, 672, 688, 1200, 1712, 2224
GQ, GK, GA, NQ, NK, Z1 = 0, 256, 512, 544, 1056, 1568
XL, GL, DQ, DK, QM, BG = 0, 768, 1536, 2304, 3072, 3584
NA_PAIRS = [(0, 0), (0, 1), (0, 2), (2, 2), (4, 2), (6, 2), (8, 3), (8, 4)]
NA_ROWS = [(0, 0, 0), (1, 0, 2), (2, 0, 4), (3, 8, 12), (4, 8, 14)]
NA_WIN = 10 * 64


def na_rows(s0, r):
    ws = min(max(r - 4, 0), 8)
    return ws - s0, ws - r + 7


def program(nc, io, stop=None):
    def scratch(name, shape):
        return nc.dram_tensor(f"scratch_{name}", list(shape), F32, kind="Internal").ap()

    Memory.held, Memory.sems, Memory.top = ExitStack(), [], 0
    with nc.semaphore("even_rows_stored") as even, nc.semaphore("odd_rows_stored") as odd, Memory.held, nc.sbuf_tensor("sbuf", [P, WORDS], F32) as whole, \
            Stage(nc, "keep") as s:
        Memory.whole, Memory.stored, Memory.stored_before = whole, (even, odd), 0
        H = s.sb("H", [P, KD, T])
        U = s.sb("U", [P, KD, T])
        ones, ident, eps = s.sb("ones", [P, P]), s.sb("ident", [P, P]), s.sb("eps", [P, 1])
        mod, gain = s.sb("mod", [P, 3 * KD, 2]), s.sb("gain", [P, KD, 2])
        load(nc, "start", [(H[:].rearrange("p k t -> p (k t)"), io["h"]), (ones[:], io["ones"]),
                           (ident[:], io["ident"]), (eps[:], io["eps"])])
        halves = [(0, NCTX, 1), (NCTX, NLAT, 0)]

        modulation(nc, "mod0", io["cc"], io["l0_w_mod"], io["l0_b_mod"], mod)
        norm_scales(nc, "scales0", io["l0_norm"], mod, gain)
        rmsnorm(nc, "norm0", H, KD, D, [(a, n, gain[:, :, v], mod[:, 0:KD, v]) for a, n, v in halves], U, ones, eps_col=eps[:])
        p0, p0v = scratch("p0", [26 * P, T]), scratch("p0v", [T, 512])
        gemm_fm(nc, "in0", U, KD, 0, T, io["l0_w_in"], 26, out_dram=p0)
        gemm_tm(nc, "in0v", U, KD, 0, T, io["l0_w_mv"], 512, p0v)

        qm, km, vm, am = scratch("qm", [768, T]), scratch("km", [512, T]), scratch("vm", [T, 512]), scratch("am", [T, 512])
        load(nc, "latents", [(U[:, k, :], p0[CQ + k * P:CQ + (k + 1) * P, :]) for k in range(5)])
        rmsnorm(nc, "qnorm", U, 3, 384, [(0, T, None, None)], U, ones, g_dram=io["l0_mla_q_norm"], eps_col=eps[:])
        rmsnorm(nc, "kvnorm", U[:, 3:5], 2, 256, [(0, T, None, None)], U[:, 3:5], ones, g_dram=io["l0_mla_kv_norm"], eps_col=eps[:])
        gemm_fm(nc, "uq", U, 3, 0, T, io["l0_w_uq"], 6, out_dram=qm)
        gemm_fm(nc, "uk", U[:, 3:5], 2, 0, T, io["l0_w_uk"], 4, out_dram=km)
        gemm_tm(nc, "uv", U[:, 3:5], 2, 0, T, io["l0_w_uv"], 512, vm)

        def v_from(rows, c0):
            src = rows.rearrange("(t p) c -> p t c", p=P)

            def issue(sp, h, tile, sem):
                sp.dma_start(tile, src[:, :, bass.ds(h * 64 + c0, 64)]).then_inc(sem, 16)
            return issue

        tile = lambda t: slice(t * P, (t + 1) * P)
        units = [Unit(tile(t), [(slice(0, NCTX), NCTX)], [0, 1], t) for t in range(2)]
        units += [Unit(tile(t), [(slice(0, T), T)], list(range(TT)), t) for t in range(2, TT)]
        attention(nc, "mla", 8, 96, 64, 96 ** -0.5, units, qm, km, v_from(vm, 0), 1, TT,
                  lambda h, u: [(0, am[u * P:(u + 1) * P, bass.ds(h * 64, 64)])], 64, ident, T, T,
                  rope=(p0[KR:KR + 32, :], io["rope"]))

        ma, mn, mf, mh = scratch("ma", [8, T]), scratch("mn", [8, T]), scratch("mf", [8, T]), scratch("mh", [512, T])
        mlstm_gates(nc, "mgates", p0[GT:GT + 16, :], io["mlstm_b"], ma, mn, mf, None)
        mlstm(nc, "mlstm", p0[MQ:MQ + 512, :], p0[MK:MK + 512, :], p0v, io["mlstm_conv"], ma, mn, mf, io["mlstm_mask"], mh, ones)
        gated_mix(nc, "mix0", am, 0, mh, 4, p0[MO:MO + 512, :], p0[Z0:Z0 + D, :], io["l0_mlstm_norm"], 0, T, 0, U, ident, ones, eps[:])
        gemm_fm(nc, "out0", U, KD, 0, T, io["l0_w_out"], KD, acc=H,
                gate=[(a, n, mod[:, 2 * KD:3 * KD, v]) for a, n, v in halves])

        modulation(nc, "mod1", io["cc"], io["l1_w_mod"], io["l1_b_mod"], mod)
        norm_scales(nc, "scales1", io["l1_norm"], mod, gain)
        rmsnorm(nc, "norm1", H, KD, D, [(a, n, gain[:, :, v], mod[:, 0:KD, v]) for a, n, v in halves], U, ones, eps_col=eps[:])
        p1, p1v = scratch("p1", [22 * P, T]), scratch("p1v", [T, 1024])
        gemm_fm(nc, "in1", U, KD, 0, T, io["l1_w_in"], 22, out_dram=p1)
        gemm_tm(nc, "in1v", U, KD, 0, T, io["l1_w_v"], 1024, p1v)
        go = scratch("go", [512, NLAT])
        gla(nc, "gla", p1[GQ:GQ + 256, :], p1[GK:GK + 256, :], p1v[:, 0:512], p1[GA:GA + 32, :], io["gla_w"], io["gla_b"],
            io["gla_keep"], io["gla_clamp"], io["gla_mask"], go, ident)

        nt = scratch("nt", [P, 4096])
        table_rows(nc, "rpb", io["rpb"], io["rpb_hot"], 33, P, 4096, nt, 8.0)
        ntv = nt.rearrange("d (c k) -> c d k", k=64)

        def na_bias(sp, h, t, sem):
            for pat, s0, r0 in NA_ROWS[:2] + [(2, 0, 4)] + NA_ROWS[3:]:
                for rr in range(2):
                    a, d0 = na_rows(s0, r0 + rr)
                    dst = t[64 * rr:64 * rr + 64, pat, NCTX + 64 * a:NCTX + 64 * (a + 8)].rearrange("c (j k) -> c j k", k=64)
                    sp.dma_start(dst, ntv[:, bass.ds(h * 16 + d0, 8), :]).then_inc(sem, 16)

        no = scratch("no", [NLAT, 512])
        units = []
        for pr, (s0, pat) in enumerate(NA_PAIRS):
            n = 8 * 64 if pat != 2 or s0 == 8 else NA_WIN
            k0 = NCTX + 64 * s0
            units.append(Unit(tile(2 + pr), [(slice(0, NCTX), NCTX), (slice(k0, k0 + n), n)],
                              [0, 1] + [k0 // P + j for j in range(n // P)], pr,
                              bias=lambda b, pat=pat, n=n: b[:, pat, 0:NCTX + n]))
        attention(nc, "na", 8, 64, 64, 64 ** -0.5, units, p1[NQ:NQ + 512, :], p1[NK:NK + 512, :], v_from(p1v, 512), 1, TT,
                  lambda h, u: [(0, no[u * P:(u + 1) * P, bass.ds(h * 64, 64)])], 64, ident, T, T,
                  bias_shape=[5, NCTX + NA_WIN], bias_load=na_bias, bias_loads=10,
                  bias_fill=[(lambda b: b[:, :, 0:NCTX], 0.0), (lambda b: b[:, :, NCTX:], NEG)])
        gated_mix(nc, "mix1", no, 4, go, 0, None, p1[Z1:Z1 + D, :], io["l1_gla_norm"], NCTX, NLAT, 0, U, ident, ones, eps[:])
        gemm_fm(nc, "out1", U, KD, NCTX, NLAT, io["l1_w_out"], KD, acc=H, gate=[(NCTX, NLAT, mod[:, 2 * KD:3 * KD, 0])])
        lat = lambda g=None: [(NCTX, NLAT, g, None)]
        rmsnorm(nc, "final1", H, KD, D, lat(), H, ones, g_dram=io["final_norm"], eps_col=eps[:])

        km2, vm2, mo2 = scratch("km2", [512, NCTX]), scratch("vm2", [NCTX, 512]), scratch("mo2", [NLAT, 512])
        load(nc, "mem", [(U[:, k, 0:NCTX], io["mem"][:, k * NCTX:(k + 1) * NCTX]) for k in range(KD)])
        rmsnorm(nc, "memnorm", U, KD, D, [(0, NCTX, None, None)], U, ones, g_dram=io["g_mem"], eps_col=eps[:])
        gemm_fm(nc, "memk", U, KD, 0, NCTX, io["w_mem_k"], 4, out_dram=km2)
        gemm_tm(nc, "memv", U, KD, 0, NCTX, io["w_mem_v"], 512, vm2)
        rmsnorm(nc, "norm2", H, KD, D, lat(), U, ones, g_dram=io["g_mix"], eps_col=eps[:])
        p2, p2v = scratch("p2", [52 * P, NLAT]), scratch("p2v", [NLAT, 768])
        gemm_fm(nc, "in2", U, KD, NCTX, NLAT, io["w_in"], 52, out_dram=p2)
        gemm_tm(nc, "in2v", U, KD, NCTX, NLAT, io["w_in_v"], 768, p2v)

        vmem = vm2.rearrange("(t p) c -> p t c", p=P)

        def mem_v(sp, h, t, sem):
            sp.dma_start(t, vmem[:, :, bass.ds(h * P, P)]).then_inc(sem, 16)

        units = [Unit(tile(t), [(slice(0, NCTX), NCTX)], [0, 1], t) for t in range(8)]
        attention(nc, "memory", 4, P, P, P ** -0.5, units, p2[QM:QM + 512, :], km2, mem_v, 1, 2,
                  lambda h, u: [(0, mo2[u * P:(u + 1) * P, bass.ds(h * P, P)])], P, ident, NLAT, NCTX)

        dt = scratch("dt", [12, 3 * 384])
        table_rows(nc, "relb", io["rel_bias"], io["rel_hot"], 33, 12, 3 * 384, dt, 8.0)
        db = [scratch(f"db{g}", [4 * P, 256]) for g in range(3)]
        spread_bias(nc, "spread", dt, scratch("dtrep", [12, P * 384]), db)
        od = scratch("od", [NLAT, 12 * 66])
        for g, dil in enumerate((1, 4, 16)):
            qr, kr = p2[DQ + 256 * g:DQ + 256 * (g + 1), :], p2[DK + 256 * g:DK + 256 * (g + 1), :]
            vg, og = p2v[:, 256 * g:256 * (g + 1)], od[:, 264 * g:264 * (g + 1)]
            whole = lambda b: b[:, 0:256]
            right = lambda b: b[:, 128:256]
            if dil < 16:
                nb = NLAT // dil // P
                vv = vg.rearrange("(b p r) c -> b p r c", p=P, r=dil)
                ov = og.rearrange("(b p r) c -> b p r c", p=P, r=dil)
                units, place = [], []
                for b in range(nb):
                    for r in range(dil):
                        a = r + dil * P * b
                        own = slice(a, a + dil * (P - 1) + 1, dil)
                        if b == 0:
                            units.append(Unit(own, [(own, P)], [r], None, bias=right))
                        else:
                            units.append(Unit(own, [(slice(a - dil * P, NLAT, dil), 2 * P)],
                                              [(b - 1) * dil + r, b * dil + r], None, bias=whole))
                        place.append((b, r))

                def load_v(sp, h, t, sem, vv=vv, nb=nb, dil=dil):
                    for b in range(nb):
                        sp.dma_start(t[:, b * dil:(b + 1) * dil, :], vv[b][:, :, bass.ds(h * 64, 64)]).then_inc(sem, 16)

                def out_rows(h, u, ov=ov, place=place):
                    b, r = place[u]
                    return [(0, ov[b][:, r, bass.ds(h * 66, 66)])]

                nv, nbias, fill = nb, 1, []
            else:
                vv = vg.rearrange("(j u r) c -> r j u c", u=8, r=2)
                ov = og.rearrange("(j u r) c -> r u j c", u=8, r=2)
                units = [Unit([slice(2 * u, NLAT, 16), slice(2 * u + 1, NLAT, 16)],
                              [(slice(2 * u, NLAT, 16), 64), (slice(2 * u + 1, NLAT, 16), 64)], [u], None,
                              bias=lambda b: b[:, 0:P]) for u in range(8)]

                def load_v(sp, h, t, sem, vv=vv):
                    for r in range(2):
                        sp.dma_start(t[64 * r:64 * r + 64], vv[r][:, :, bass.ds(h * 64, 64)]).then_inc(sem, 16)

                def out_rows(h, u, ov=ov):
                    return [(64 * r, ov[r][u][:, bass.ds(h * 66, 66)]) for r in range(2)]

                nv, nbias, fill = 2, 2, [(lambda b: b[:, 0:256], NEG)]
            attention(nc, f"dil{dil}", 4, 64, 64, 64 ** -0.5, units, qr, kr, load_v, nv, 8, out_rows, 66, ident,
                      NLAT, NLAT, stats=True, bias_shape=[256], bias_load=dil_bias(db, g), bias_loads=nbias,
                      bias_fill=fill)

        dm = scratch("dm", [NLAT, 256])
        combine_groups(nc, "groups", od, dm)

        spd, yl = scratch("spd", [768, 1]), scratch("yl", [768, NLAT])
        with Stage(nc, "lam") as s2:
            spc = s2.sb("spc", [P, 6])
            softplus_column(nc, "softplus", io["lam"], 6, spc)
            st = s2.sem("stored")
            with nc.Block() as block:
                @block.sync
                def _(sp):
                    sp.dma_start(spd.rearrange("(j p) o -> p (j o)", p=P), spc[:], allow_slow_non_contiguous=True).then_inc(st, 16)
                    sp.wait_ge(st, 16)
        rg_lru(nc, "lru", p2[XL:XL + 768, :], p2[GL:GL + 768, :], io["lru_par"], io["w_rg_a"], io["w_rg_x"], spd, yl)

        yb = scratch("yb", [3 * D, NLAT])
        load(nc, "ylru", [(U[:, k, 0:NLAT], yl[k * P:(k + 1) * P, :]) for k in range(6)])
        gemm_fm(nc, "lruout", U, 6, 0, NLAT, io["w_lru_out"], KD, out_dram=yb[0:D, :])
        to_features(nc, "dilT", dm, 8, 256, U, ident)
        gemm_fm(nc, "dilout", U, 2, 0, NLAT, io["w_dil_out"], KD, out_dram=yb[D:2 * D, :])
        to_features(nc, "memT", mo2, 8, 512, U, ident)
        gemm_fm(nc, "memout", U, 4, 0, NLAT, io["w_mem_out"], KD, out_dram=yb[2 * D:3 * D, :])
        merge_branches(nc, "merge", p2[BG:BG + 3 * D, :], io["b_gate"], yb, U)
        gemm_fm(nc, "out2", U, KD, NCTX, NLAT, io["w_out"], KD, acc=H, gate=[(NCTX, NLAT, None)])

        rmsnorm(nc, "mlpnorm", H, KD, D, lat(), U, ones, g_dram=io["g_mlp"], eps_col=eps[:])
        with Stage(nc, "mlp") as s2:
            hid = s2.sb("hid", [P, KD, NLAT])
            for f in range(4):
                gemm_fm(nc, f"up{f}", U, KD, NCTX, NLAT, io["w_mlp_in"][f * D:(f + 1) * D, :], KD, out_sb=hid, relu2=True)
                gemm_fm(nc, f"down{f}", hid, KD, 0, NLAT, io["w_mlp_out"][f * D:(f + 1) * D, :], KD, acc=H[:, :, NCTX:T],
                        gate=[(0, NLAT, None)])
        rmsnorm(nc, "final2", H, KD, D, lat(), H, ones, g_dram=io["g_final"], eps_col=eps[:])
        load(nc, "end", [(io["out"][k * P:(k + 1) * P, :], H[:, k, NCTX:T]) for k in range(KD)])


def dil_bias(db, g):
    def issue(sp, h, t, sem):
        if g < 2:
            sp.dma_start(t, db[g][bass.ds(h * P, P), :]).then_inc(sem, 16)
        else:
            for r in range(2):
                sp.dma_start(t[64 * r:64 * r + 64, 64 * r:64 * r + 64], db[g][bass.ds(h * P, 64), 0:64]).then_inc(sem, 16)
    return issue


def spread_bias(nc, name, dt, rep, db):
    with Stage(nc, name) as s:
        copied, done = s.sem("copied"), s.sem("done")
        block = s.block()

        @block.sync
        def _(sp):
            for h in range(12):
                sp.dma_start(rep[h:h + 1, :].rearrange("a (q y) -> (a q) y", y=384),
                             dt[h:h + 1, h // 4 * 384:h // 4 * 384 + 384].broadcast_to([P, 384])).then_inc(copied, 16)
            sp.wait_ge(copied, 16 * 12)
            for g in range(3):
                n, w, y0 = (P, 256, 127) if g < 2 else (64, 64, 255)
                for h in range(4):
                    src = bass.AP(rep.tensor, (4 * g + h) * P * 384 + y0, [[383, n], [1, w]])
                    sp.dma_start(db[g][h * P:h * P + n, 0:w], src).then_inc(done, 16)
            sp.wait_ge(done, 16 * 12)
def _pad_cols(w, n):
    return np.concatenate([w, np.zeros((w.shape[0], n - w.shape[1]), w.dtype)], 1) if n > w.shape[1] else w


def tile_fm(w, mult=2):
    K, M = w.shape
    mt = -(-M // P)
    mt += -mt % mult
    w = _pad_cols(w, mt * P).reshape(K // P, P, mt, P)
    return np.ascontiguousarray(w.transpose(2, 1, 0, 3)).reshape(mt * P, K)


def tile_tm(w):
    K, n = w.shape
    return np.ascontiguousarray(w.reshape(K // P, P, n).transpose(1, 0, 2)).reshape(P, -1)


def cols(v):
    return np.ascontiguousarray(v.reshape(-1, P).T)


def onehots():
    c, k = np.meshgrid(np.arange(64), np.arange(64), indexing="ij")
    w0 = np.clip(c - 8, 0, 48)
    ok = (k >= w0) & (k < w0 + 16)
    hot = np.zeros((33, 64, 64), np.float32)
    for j in range(31):
        hot[j] = ok & (k - c + 15 == j)
    hot[31] = np.where(ok, 0.0, NEG)
    hot[32] = NEG
    rel = np.zeros((33, 3, 384), np.float32)
    for g, dil in enumerate((1, 4, 16)):
        off = 255 - np.arange(384)
        dist = np.maximum(off, 0) * dil
        df = np.maximum(dist, 1).astype(np.float32)
        large = 16 + (np.log(df / np.float32(16)) / np.float32(math.log(2048 / 16)) * np.float32(16)).astype(np.int32)
        bucket = np.where(dist < 16, dist, np.minimum(large, 31))
        valid = (off >= 0) & (off <= 128)
        for j in range(32):
            rel[j, g] = valid & (bucket == j)
        rel[32, g] = np.where(valid, 0.0, NEG)
    return hot.reshape(33, -1), rel.reshape(33, -1)


def rope_rows():
    t = np.arange(NLAT)
    inv = (1.0 / (np.float32(10000.0) ** (np.arange(8, dtype=np.float32) / np.float32(8)))).astype(np.float32)
    ang = np.stack([(t // 64)[None, :].astype(np.float32) * inv[:, None], (t % 64)[None, :].astype(np.float32) * inv[:, None]])
    cos, sin = np.ones((2, 2, 8, T), np.float32), np.zeros((2, 2, 8, T), np.float32)
    cos[:, :, :, NCTX:] = np.cos(ang)[:, None]
    sin[:, 0, :, NCTX:] = -np.sin(ang)
    sin[:, 1, :, NCTX:] = np.sin(ang)
    return np.concatenate([cos.reshape(32, T), sin.reshape(32, T)])


def layout(a):
    a = {k: np.asarray(v) for k, v in a.items()}
    f = np.float32
    o = {}
    tok = np.concatenate([a["ctx"][0], a["x"][0]], 0)

    def feat(x):
        return np.ascontiguousarray(x.T.reshape(-1, P, x.shape[0]).transpose(1, 0, 2)).reshape(P, -1)

    o["h"], o["mem"] = feat(tok), feat(a["mem_2"][0])
    o["cc"] = feat(np.stack([a["c"][0], a["c_ctx"]]))
    o["ones"], o["ident"], o["eps"] = np.ones((P, P), f), np.eye(P, dtype=f), np.full((P, 1), EPS, f)
    for layer in ("l0", "l1"):
        o[f"{layer}_w_mod"] = tile_fm(a[f"{layer}_w_mod"])
        o[f"{layer}_b_mod"], o[f"{layer}_norm"] = cols(a[f"{layer}_b_mod"]), cols(a[f"{layer}_norm"])
        o[f"{layer}_w_out"] = tile_fm(a[f"{layer}_w_out"])
    w = a["l0_w_in"]
    g = w[:, 2720:2736].reshape(D, 2, 2, 4).transpose(0, 2, 1, 3).reshape(D, 16)
    o["l0_w_in"] = tile_fm(np.concatenate([w[:, 0:672], g, w[:, 672:1696], w[:, 2208:2720], w[:, 2736:3760]], 1))
    o["l0_w_mv"] = tile_tm(w[:, 1696:2208])
    o["l0_w_uq"] = tile_fm(a["l0_mla_w_uq"])
    kv = a["l0_mla_w_ukv"].reshape(256, 8, 2, 64)
    o["l0_w_uk"], o["l0_w_uv"] = tile_fm(kv[:, :, 0].reshape(256, 512)), tile_tm(kv[:, :, 1].reshape(256, 512))
    for n in ("l0_mla_q_norm", "l0_mla_kv_norm", "l0_mlstm_norm", "l1_gla_norm", "final_norm"):
        o[n] = cols(a[n])
    o["rope"] = rope_rows()
    o["mlstm_b"] = np.concatenate([a["l0_mlstm_b_i"].T, a["l0_mlstm_b_f"].T], 1)
    o["mlstm_conv"] = np.concatenate([a["l0_mlstm_conv_w"], a["l0_mlstm_conv_b"][None]], 0).T
    o["mlstm_mask"] = mlstm_masks()
    w = a["l1_w_in"]
    o["l1_w_in"] = tile_fm(np.concatenate([w[:, 0:512], w[:, 1024:2080], w[:, 2592:3616]], 1))
    o["l1_w_v"] = tile_tm(np.concatenate([w[:, 512:1024], w[:, 2080:2592]], 1))
    o["gla_w"], o["gla_b"] = a["l1_gla_w_gate"].reshape(32, 256), a["l1_gla_b_gate"].T
    o["gla_keep"], o["gla_clamp"], o["gla_mask"] = gla_consts()
    rpb = np.zeros((33, 8, 16), f)
    rpb[0:31, :, 0:15] = a["l1_na_rpb"].transpose(2, 0, 1)
    rpb[31] = 1.0
    rpb[32, :, 15] = 1.0
    o["rpb"] = rpb.reshape(33, P)
    o["rpb_hot"], o["rel_hot"] = onehots()
    o["rel_bias"] = np.concatenate([a["rel_bias_2"], np.ones((1, 12), f)])
    o["g_mem"], o["g_mix"], o["g_mlp"], o["g_final"] = (cols(a[n]) for n in ("g_mem_2", "g_mix_2", "g_mlp_2", "g_final_2"))
    o["w_mem_k"], o["w_mem_v"] = tile_fm(a["w_mem_kv_2"][:, 0:512]), tile_tm(a["w_mem_kv_2"][:, 512:1024])
    w = a["w_in_2"]
    o["w_in"] = tile_fm(np.concatenate([w[:, 0:3072], w[:, 3840:7424]], 1))
    o["w_in_v"] = tile_tm(w[:, 3072:3840])
    o["b_gate"] = cols(a["b_gate_2"])
    o["lru_par"] = np.concatenate([a["conv_w_2"], a["conv_b_2"][None], a["b_rg_a_2"][None], a["b_rg_x_2"][None],
                                   np.zeros((1, 768), f)]).T
    o["lam"] = cols(a["lru_lambda_2"])
    for n in ("w_rg_a", "w_rg_x"):
        b = np.zeros((6, 2, 64, 2, 64), f)
        for r in range(2):
            b[:, r, :, r, :] = a[n + "_2"].reshape(6, 2, 64, 64)[:, r]
        o[n] = b.reshape(768, P)
    for n in ("w_lru_out", "w_dil_out", "w_mem_out", "w_out", "w_mlp_in"):
        o[n] = tile_fm(a[n + "_2"])
    o["w_mlp_out"] = np.concatenate([tile_fm(a["w_mlp_out_2"][f0 * D:(f0 + 1) * D]) for f0 in range(4)])
    return {n: np.ascontiguousarray(v) for n, v in o.items()}


def kernel(**inputs):
    import concourse.bacc as _bacc
    from concourse.bass_utils import run_bass_kernel_spmd as _run

    nc = _bacc.Bacc("TRN2", target_bir_lowering=False, num_devices=1)
    arrays = {f"in_{n}": v for n, v in layout(inputs).items()}
    io = {n[3:]: nc.dram_tensor(n, list(v.shape), mybir.dt.from_np(v.dtype), kind="ExternalInput").ap()
          for n, v in arrays.items()}
    io["out"] = nc.dram_tensor("out_0", [D, NLAT], F32, kind="ExternalOutput").ap()
    program(nc, io)
    r = _run(nc, [arrays], core_ids=[0])
    return np.ascontiguousarray(r.results[0]["out_0"].T)[None]
```
